# Optimizing a Trainium2 kernel written in Bass

```python
import math
import jax, jax.numpy as jnp
from jax import lax
import numpy as np

D_MODEL = 2048
BATCH = 1
SEQ = 256
DEPTH = 1

Q_BLOCK = 128
ROPE_THETA = 10000.0
NORM_EPS = 1e-6

MLA_HEADS = 8
MLA_NOPE_DIM = 128
MLA_ROPE_DIM = 64
MLA_V_DIM = 128
MLA_Q_LORA = 512
MLA_KV_LORA = 256
MLA_OUT = MLA_HEADS * MLA_V_DIM

DIFF_HEADS = 4
DIFF_HEAD_DIM = 128
DIFF_V_DIM = 2 * DIFF_HEAD_DIM
DIFF_W = DIFF_HEADS * 2 * DIFF_HEAD_DIM
DIFF_OUT = DIFF_HEADS * DIFF_V_DIM

MIX_WIDTH = MLA_OUT + DIFF_OUT

IN_SPLITS = (MLA_Q_LORA, MLA_KV_LORA, MLA_ROPE_DIM, DIFF_W, DIFF_W, DIFF_W)
IN_WIDTH = sum(IN_SPLITS)

MEM_TOKENS = 256
X_HEADS = 4
X_HEAD_DIM = 128
X_WIDTH = X_HEADS * X_HEAD_DIM

FFN_HIDDEN = int(math.ceil(8 * D_MODEL / 3 / 256) * 256)


def rms_norm(x, g, eps=NORM_EPS):
    xf = x.astype(jnp.float32)
    y = xf * lax.rsqrt(jnp.mean(xf * xf, axis=-1, keepdims=True) + eps)
    return (y * g.astype(jnp.float32)).astype(x.dtype)

def rope_tables(positions, dim):
    inv_freq = ROPE_THETA ** (-jnp.arange(0, dim, 2, dtype=jnp.float32) / dim)
    ang = positions.astype(jnp.float32)[..., None] * inv_freq
    return jnp.cos(ang), jnp.sin(ang)

def apply_rope(t, cos, sin):
    shp = cos.shape[:2] + (1,) * (t.ndim - 3) + cos.shape[-1:]
    c, s = cos.reshape(shp), sin.reshape(shp)
    half = t.shape[-1] // 2
    t1 = t[..., :half].astype(jnp.float32)
    t2 = t[..., half:].astype(jnp.float32)
    return jnp.concatenate([t1 * c - t2 * s, t1 * s + t2 * c], axis=-1).astype(t.dtype)

def _to_blocks(t):
    b, s = t.shape[:2]
    return jnp.moveaxis(t.reshape((b, s // Q_BLOCK, Q_BLOCK) + t.shape[2:]), 1, 0)

def _from_blocks(t):
    t = jnp.moveaxis(t, 0, 1)
    return t.reshape((t.shape[0], t.shape[1] * t.shape[2]) + t.shape[3:])

def mla_attention(q_nope, q_rope, k_nope, k_rope, v):
    scale = (MLA_NOPE_DIM + MLA_ROPE_DIM) ** -0.5

    def block(qs):
        qn_b, qr_b = qs
        s = (jnp.einsum('bqhd,bkhd->bhqk', qn_b, k_nope)
             + jnp.einsum('bqhr,bkr->bhqk', qr_b, k_rope))
        p = jax.nn.softmax(s.astype(jnp.float32) * scale, axis=-1).astype(v.dtype)
        return jnp.einsum('bhqk,bkhd->bqhd', p, v)

    return _from_blocks(lax.map(block, (_to_blocks(q_nope), _to_blocks(q_rope))))

def diff_attention(q1, q2, k1, k2, v, lam):
    scale = DIFF_HEAD_DIM ** -0.5

    def block(qs):
        q1_b, q2_b = qs
        p1 = jax.nn.softmax(jnp.einsum('bqhd,bkhd->bhqk', q1_b, k1).astype(jnp.float32) * scale, axis=-1)
        p2 = jax.nn.softmax(jnp.einsum('bqhd,bkhd->bhqk', q2_b, k2).astype(jnp.float32) * scale, axis=-1)
        p = (p1 - lam * p2).astype(v.dtype)
        return jnp.einsum('bhqk,bkhe->bqhe', p, v)

    return _from_blocks(lax.map(block, (_to_blocks(q1), _to_blocks(q2))))

def first_inputs(seed: int = 0) -> dict:
    key = jax.random.key(seed)
    ks = iter(jax.random.split(key, 40))

    def dense(shape):
        return jax.random.normal(next(ks), shape, jnp.float32) * (shape[-2] ** -0.5)

    def gain(n):
        return 1.0 + 0.02 * jax.random.normal(next(ks), (DEPTH, n), jnp.float32)

    x = jax.random.normal(next(ks), (BATCH, SEQ, D_MODEL), jnp.float32)
    mem = jax.random.normal(next(ks), (BATCH, MEM_TOKENS, D_MODEL), jnp.float32)
    offsets = jax.random.randint(next(ks), (BATCH, 1), 0, 1024, dtype=jnp.int32)
    positions = jnp.arange(SEQ, dtype=jnp.int32)[None, :] + offsets

    return {
        "x": x,
        "mem": mem,
        "positions": positions,
        "g_mix": gain(D_MODEL),
        "w_in": dense((DEPTH, D_MODEL, IN_WIDTH)),
        "g_q_lat": gain(MLA_Q_LORA),
        "w_uq": dense((DEPTH, MLA_Q_LORA, MLA_HEADS * (MLA_NOPE_DIM + MLA_ROPE_DIM))),
        "g_kv_lat": gain(MLA_KV_LORA),
        "w_ukv": dense((DEPTH, MLA_KV_LORA, MLA_HEADS * (MLA_NOPE_DIM + MLA_V_DIM))),
        "lambda_q1": 0.1 * jax.random.normal(next(ks), (DEPTH, DIFF_HEAD_DIM), jnp.float32),
        "lambda_k1": 0.1 * jax.random.normal(next(ks), (DEPTH, DIFF_HEAD_DIM), jnp.float32),
        "lambda_q2": 0.1 * jax.random.normal(next(ks), (DEPTH, DIFF_HEAD_DIM), jnp.float32),
        "lambda_k2": 0.1 * jax.random.normal(next(ks), (DEPTH, DIFF_HEAD_DIM), jnp.float32),
        "g_diff_sub": gain(DIFF_V_DIM),
        "w_out": dense((DEPTH, MIX_WIDTH, D_MODEL)),
        "g_xattn": gain(D_MODEL),
        "g_mem": gain(D_MODEL),
        "w_xq": dense((DEPTH, D_MODEL, X_WIDTH)),
        "w_xk": dense((DEPTH, D_MODEL, X_WIDTH)),
        "w_xv": dense((DEPTH, D_MODEL, X_WIDTH)),
        "w_xo": dense((DEPTH, X_WIDTH, D_MODEL)),
        "g_ffn": gain(D_MODEL),
        "w_gate": dense((DEPTH, D_MODEL, FFN_HIDDEN)),
        "w_up": dense((DEPTH, D_MODEL, FFN_HIDDEN)),
        "w_down": dense((DEPTH, FFN_HIDDEN, D_MODEL)),
        "g_final": 1.0 + 0.02 * jax.random.normal(next(ks), (D_MODEL,), jnp.float32),
    }

def first_block(x, mem, positions, g_mix, w_in, g_q_lat, w_uq, g_kv_lat, w_ukv,
              lambda_q1, lambda_k1, lambda_q2, lambda_k2, g_diff_sub, w_out,
              g_xattn, g_mem, w_xq, w_xk, w_xv, w_xo,
              g_ffn, w_gate, w_up, w_down, g_final):
    b, s, _ = x.shape
    m_len = mem.shape[1]
    cos_r, sin_r = rope_tables(positions, MLA_ROPE_DIM)
    cos_d, sin_d = rope_tables(positions, DIFF_HEAD_DIM)
    split_pts = [int(v) for v in np.cumsum(IN_SPLITS)[:-1]]

    for layer in range(DEPTH):
        h = rms_norm(x, g_mix[layer])
        proj = h @ w_in[layer]
        c_q, c_kv, k_rope, dq, dk, dv = jnp.split(proj, split_pts, axis=-1)

        q = (rms_norm(c_q, g_q_lat[layer]) @ w_uq[layer]).reshape(b, s, MLA_HEADS, MLA_NOPE_DIM + MLA_ROPE_DIM)
        q_nope = q[..., :MLA_NOPE_DIM]
        q_rope = apply_rope(q[..., MLA_NOPE_DIM:], cos_r, sin_r)
        kv = (rms_norm(c_kv, g_kv_lat[layer]) @ w_ukv[layer]).reshape(b, s, MLA_HEADS, MLA_NOPE_DIM + MLA_V_DIM)
        k_nope, v_mla = kv[..., :MLA_NOPE_DIM], kv[..., MLA_NOPE_DIM:]
        k_rope = apply_rope(k_rope, cos_r, sin_r)
        out_mla = mla_attention(q_nope, q_rope, k_nope, k_rope, v_mla).reshape(b, s, MLA_OUT)

        dq = apply_rope(dq.reshape(b, s, DIFF_HEADS, 2, DIFF_HEAD_DIM), cos_d, sin_d)
        dk = apply_rope(dk.reshape(b, s, DIFF_HEADS, 2, DIFF_HEAD_DIM), cos_d, sin_d)
        dv = dv.reshape(b, s, DIFF_HEADS, DIFF_V_DIM)
        lambda_init = 0.8 - 0.6 * math.exp(-0.3 * layer)
        lam = (jnp.exp(jnp.sum(lambda_q1[layer].astype(jnp.float32) * lambda_k1[layer].astype(jnp.float32)))
               - jnp.exp(jnp.sum(lambda_q2[layer].astype(jnp.float32) * lambda_k2[layer].astype(jnp.float32)))
               + lambda_init)
        o_diff = diff_attention(dq[..., 0, :], dq[..., 1, :], dk[..., 0, :], dk[..., 1, :], dv, lam)
        o_diff = rms_norm(o_diff, g_diff_sub[layer], eps=1e-5) * (1.0 - lambda_init)
        out_diff = o_diff.reshape(b, s, DIFF_OUT)

        x = x + jnp.concatenate([out_mla, out_diff], axis=-1) @ w_out[layer]

        hx = rms_norm(x, g_xattn[layer])
        hm = rms_norm(mem, g_mem[layer])
        xq = (hx @ w_xq[layer]).reshape(b, s, X_HEADS, X_HEAD_DIM)
        xk = (hm @ w_xk[layer]).reshape(b, m_len, X_HEADS, X_HEAD_DIM)
        xv = (hm @ w_xv[layer]).reshape(b, m_len, X_HEADS, X_HEAD_DIM)
        sc = jnp.einsum('bqhd,bkhd->bhqk', xq, xk).astype(jnp.float32) * (X_HEAD_DIM ** -0.5)
        p = jax.nn.softmax(sc, axis=-1).astype(xv.dtype)
        xo = jnp.einsum('bhqk,bkhd->bqhd', p, xv).reshape(b, s, X_WIDTH)
        x = x + xo @ w_xo[layer]

        hf = rms_norm(x, g_ffn[layer])
        x = x + (jax.nn.silu(hf @ w_gate[layer]) * (hf @ w_up[layer])) @ w_down[layer]

    return rms_norm(x, g_final)


PLE_DIM = 256
HEAD_DIM = 128
ATTN_HEADS = 8
RET_HEADS = 8
ATTN_WIDTH = ATTN_HEADS * HEAD_DIM
RET_WIDTH = RET_HEADS * HEAD_DIM
MIX_WIDTH_2 = ATTN_WIDTH + RET_WIDTH
IN_COLS = 3 * ATTN_WIDTH + 4 * RET_WIDTH
D_FF = -(-(8 * D_MODEL) // (3 * 256)) * 256
MOBA_BLOCK = 256
MOBA_TOPK = 3
MOBA_Q_CHUNK = 32
RET_CHUNK = 128
RMS_EPS = 1e-6
NEG_INF = -1e30


def rms_norm_2(x, g):
    xf = x.astype(jnp.float32)
    y = xf * lax.rsqrt(jnp.mean(xf * xf, axis=-1, keepdims=True) + RMS_EPS)
    return (y * g.astype(jnp.float32)).astype(x.dtype)

def rotate_half_split(x, pos, inv_freq):
    ang = pos[:, None] * inv_freq[None, :]
    cos = jnp.cos(ang).astype(x.dtype)
    sin = jnp.sin(ang).astype(x.dtype)
    x1, x2 = jnp.split(x, 2, axis=-1)
    return jnp.concatenate([x1 * cos - x2 * sin, x2 * cos + x1 * sin], axis=-1)

def moba_attention(q, k, v):
    B, H, T, d = q.shape
    BS = MOBA_BLOCK
    QC = MOBA_Q_CHUNK
    NB = -(-T // BS)
    Tp = NB * BS
    NC = T // QC
    K_SEL = min(MOBA_TOPK, max(NB - 1, 1))
    scale = 1.0 / np.sqrt(d)

    pad = ((0, 0), (0, 0), (0, Tp - T), (0, 0))
    kb = jnp.pad(k, pad).reshape(B, H, NB, BS, d)
    vb = jnp.pad(v, pad).reshape(B, H, NB, BS, d)

    k_mean = jnp.mean(kb.astype(jnp.float32), axis=3)
    gate = jnp.einsum('bhtd,bhnd->bhtn', q.astype(jnp.float32), k_mean)
    q_block = jnp.arange(T) // BS
    past = jnp.arange(NB)[None, :] < q_block[:, None]
    gate = jnp.where(past[None, None], gate, NEG_INF)
    _, sel_idx = lax.top_k(gate, K_SEL)

    b_idx = jnp.arange(B)[:, None, None, None]
    h_idx = jnp.arange(H)[None, :, None, None]

    def chunk_step(args):
        c, q_c, idx_c = args
        t = c * QC + jnp.arange(QC)
        kg = kb[b_idx, h_idx, idx_c].reshape(B, H, QC, K_SEL * BS, d)
        vg = vb[b_idx, h_idx, idx_c].reshape(B, H, QC, K_SEL * BS, d)
        valid = jnp.arange(K_SEL)[None, :] < (t // BS)[:, None]
        valid = jnp.repeat(valid, BS, axis=1)
        s_sel = jnp.einsum('bhqd,bhqnd->bhqn', q_c, kg).astype(jnp.float32) * scale
        s_sel = jnp.where(valid[None, None], s_sel, NEG_INF)
        b0 = (c * QC) // BS
        k_own = lax.dynamic_index_in_dim(kb, b0, axis=2, keepdims=False)
        v_own = lax.dynamic_index_in_dim(vb, b0, axis=2, keepdims=False)
        key_pos = b0 * BS + jnp.arange(BS)
        causal = key_pos[None, :] <= t[:, None]
        s_own = jnp.einsum('bhqd,bhkd->bhqk', q_c, k_own).astype(jnp.float32) * scale
        s_own = jnp.where(causal[None, None], s_own, NEG_INF)
        probs = jax.nn.softmax(jnp.concatenate([s_sel, s_own], axis=-1), axis=-1)
        p_sel = probs[..., :K_SEL * BS].astype(v.dtype)
        p_own = probs[..., K_SEL * BS:].astype(v.dtype)
        return (jnp.einsum('bhqn,bhqnd->bhqd', p_sel, vg)
                + jnp.einsum('bhqk,bhkd->bhqd', p_own, v_own))

    q_ch = jnp.moveaxis(q.reshape(B, H, NC, QC, d), 2, 0)
    idx_ch = jnp.moveaxis(sel_idx.reshape(B, H, NC, QC, K_SEL), 2, 0)
    out = lax.map(chunk_step, (jnp.arange(NC), q_ch, idx_ch))
    return jnp.moveaxis(out, 0, 2).reshape(B, H, T, d)

def retention_chunkwise(q, k, v):
    B, H, T, d = q.shape
    dv = v.shape[-1]
    C = RET_CHUNK
    N = T // C
    log_g = jnp.log(1.0 - jnp.power(2.0, -5.0 - jnp.arange(H, dtype=jnp.float32)))
    j = jnp.arange(C, dtype=jnp.float32)
    rel = j[:, None] - j[None, :]
    decay = jnp.where(rel >= 0, jnp.exp(log_g[:, None, None] * jnp.maximum(rel, 0.0)), 0.0)

    qc = q.reshape(B, H, N, C, d)
    kc = k.reshape(B, H, N, C, d)
    vc = v.reshape(B, H, N, C, dv)

    s = jnp.einsum('bhncd,bhnmd->bhncm', qc, kc) * decay[None, :, None]
    intra = jnp.einsum('bhncm,bhnme->bhnce', s, vc)

    k_dec = kc * jnp.exp(log_g[:, None] * (C - 1.0 - j)[None, :])[None, :, None, :, None]
    U = jnp.einsum('bhncd,bhnce->nbhde', k_dec, vc)
    g_chunk = jnp.exp(log_g * C)[None, :, None, None]

    def step(S, U_n):
        return g_chunk * S + U_n, S

    _, S_prev = lax.scan(step, jnp.zeros((B, H, d, dv), jnp.float32), U)
    q_dec = qc * jnp.exp(log_g[:, None] * (j + 1.0)[None, :])[None, :, None, :, None]
    cross = jnp.einsum('bhncd,nbhde->bhnce', q_dec, S_prev)
    return (intra + cross).reshape(B, H, T, dv)

def second_inputs(seed: int = 0) -> dict:
    key = jax.random.key(seed)
    ks = jax.random.split(key, 20)
    f32 = jnp.float32
    nrm = lambda k, shape, fan: jax.random.normal(k, shape, f32) * (fan ** -0.5)
    gain = lambda k, shape: 1.0 + 0.05 * jax.random.normal(k, shape, f32)
    return {
        "x": jax.random.normal(ks[0], (BATCH, SEQ, D_MODEL), f32),
        "p": jax.random.normal(ks[1], (DEPTH, BATCH, SEQ, PLE_DIM), f32),
        "g_mix": gain(ks[2], (DEPTH, D_MODEL)),
        "w_in": nrm(ks[3], (DEPTH, D_MODEL, IN_COLS), D_MODEL),
        "q_norm": gain(ks[4], (DEPTH, HEAD_DIM)),
        "k_norm": gain(ks[5], (DEPTH, HEAD_DIM)),
        "g_ret": gain(ks[6], (DEPTH, RET_WIDTH)),
        "w_o": nrm(ks[7], (DEPTH, MIX_WIDTH_2, D_MODEL), MIX_WIDTH_2),
        "g_ffn": gain(ks[8], (DEPTH, D_MODEL)),
        "w_gate": nrm(ks[9], (DEPTH, D_MODEL, D_FF), D_MODEL),
        "w_up": nrm(ks[10], (DEPTH, D_MODEL, D_FF), D_MODEL),
        "w_down": nrm(ks[11], (DEPTH, D_FF, D_MODEL), D_FF),
        "g_ple": gain(ks[12], (DEPTH, D_MODEL)),
        "w_ple_gate": nrm(ks[13], (DEPTH, D_MODEL, D_MODEL), D_MODEL),
        "b_ple_gate": 0.01 * jax.random.normal(ks[14], (DEPTH, D_MODEL), f32),
        "w_ple_proj": nrm(ks[15], (DEPTH, PLE_DIM, D_MODEL), PLE_DIM),
    }

def second_block(x, p, g_mix, w_in, q_norm, k_norm, g_ret, w_o, g_ffn, w_gate, w_up,
              w_down, g_ple, w_ple_gate, b_ple_gate, w_ple_proj):
    B, T, _ = x.shape
    pos = jnp.arange(T, dtype=jnp.float32)
    inv_freq_attn = jnp.power(ROPE_THETA, -jnp.arange(0, HEAD_DIM, 2, dtype=jnp.float32) / HEAD_DIM)
    inv_freq_ret = jnp.power(ROPE_THETA, -jnp.linspace(0.0, 1.0, HEAD_DIM // 2, dtype=jnp.float32))
    split_at = np.cumsum([ATTN_WIDTH] * 3 + [RET_WIDTH] * 3).tolist()

    def heads(t, n):
        return t.reshape(B, T, n, HEAD_DIM).transpose(0, 2, 1, 3)

    for i in range(DEPTH):
        h = rms_norm_2(x, g_mix[i])
        z = h @ w_in[i]
        aq, ak, av, rq, rk, rv, rg = jnp.split(z, split_at, axis=-1)

        aq = rotate_half_split(heads(rms_norm_2(aq.reshape(B, T, ATTN_HEADS, HEAD_DIM), q_norm[i]).reshape(B, T, ATTN_WIDTH), ATTN_HEADS), pos, inv_freq_attn)
        ak = rotate_half_split(heads(rms_norm_2(ak.reshape(B, T, ATTN_HEADS, HEAD_DIM), k_norm[i]).reshape(B, T, ATTN_WIDTH), ATTN_HEADS), pos, inv_freq_attn)
        a_out = moba_attention(aq, ak, heads(av, ATTN_HEADS))
        a_out = a_out.transpose(0, 2, 1, 3).reshape(B, T, ATTN_WIDTH)

        rq_h = rotate_half_split(heads(rq, RET_HEADS), pos, inv_freq_ret).astype(jnp.float32)
        rk_h = (rotate_half_split(heads(rk, RET_HEADS), pos, inv_freq_ret).astype(jnp.float32)
                * (HEAD_DIM ** -0.5))
        r = retention_chunkwise(rq_h, rk_h, heads(rv, RET_HEADS).astype(jnp.float32))
        r = r * lax.rsqrt(jnp.mean(r * r, axis=-1, keepdims=True) + RMS_EPS)
        r = r.transpose(0, 2, 1, 3).reshape(B, T, RET_WIDTH) * g_ret[i].astype(jnp.float32)
        r_out = (jax.nn.silu(rg.astype(jnp.float32)) * r).astype(x.dtype)

        x = x + jnp.concatenate([a_out, r_out], axis=-1) @ w_o[i]

        h2 = rms_norm_2(x, g_ffn[i])
        x = x + (jax.nn.silu(h2 @ w_gate[i]) * (h2 @ w_up[i])) @ w_down[i]

        gate = jax.nn.sigmoid(rms_norm_2(x, g_ple[i]) @ w_ple_gate[i] + b_ple_gate[i])
        x = x + (p[i] @ w_ple_proj[i]) * gate
    return x


def setup_inputs(seed=0):
    out = dict(first_inputs(seed))
    for name, value in second_inputs(seed + 1).items():
        if name != "x":
            out[name + "_2"] = value
    return out


def reference(
    x, mem, positions, g_mix, w_in, g_q_lat, w_uq, g_kv_lat, w_ukv, lambda_q1, lambda_k1,
    lambda_q2, lambda_k2, g_diff_sub, w_out, g_xattn, g_mem, w_xq, w_xk, w_xv, w_xo, g_ffn,
    w_gate, w_up, w_down, g_final, p_2, g_mix_2, w_in_2, q_norm_2, k_norm_2, g_ret_2, w_o_2,
    g_ffn_2, w_gate_2, w_up_2, w_down_2, g_ple_2, w_ple_gate_2, b_ple_gate_2, w_ple_proj_2,
):
    x = first_block(
        x, mem, positions, g_mix, w_in, g_q_lat, w_uq, g_kv_lat, w_ukv, lambda_q1, lambda_k1,
        lambda_q2, lambda_k2, g_diff_sub, w_out, g_xattn, g_mem, w_xq, w_xk, w_xv, w_xo, g_ffn,
        w_gate, w_up, w_down, g_final,
    )
    return second_block(
        x, p_2, g_mix_2, w_in_2, q_norm_2, k_norm_2, g_ret_2, w_o_2, g_ffn_2, w_gate_2, w_up_2,
        w_down_2, g_ple_2, w_ple_gate_2, b_ple_gate_2, w_ple_proj_2,
    )


_drawn_inputs = setup_inputs


def setup_inputs(seed=0):
    import zlib

    import numpy as np

    out = dict(_drawn_inputs(seed))
    spreads = {}
    factors = {'g_q_lat': 8.0,
     'g_kv_lat': 8.0,
     'g_diff_sub': 3.783,
     'g_xattn': 8.0,
     'g_mem': 8.0,
     'g_ffn': 3.384,
     'q_norm_2': 8.0,
     'k_norm_2': 8.0,
     'g_ret_2': 2.997,
     'g_ple_2': 22.25,
     'b_ple_gate_2': 200.0}
    for name, (base, spread) in spreads.items():
        noise = np.random.default_rng([zlib.crc32(name.encode()), seed]).standard_normal(out[name].shape)
        drawn = base * np.exp(spread * noise) if base else spread * noise
        out[name] = __import__('jax').numpy.asarray(drawn.astype(out[name].dtype))
    for name, factor in factors.items():
        out[name] = (out[name] * factor).astype(out[name].dtype)
    return out
```

```python
from contextlib import ExitStack, contextmanager

import numpy as np

import concourse.bass as bass
from concourse import mybir

F32 = mybir.dt.float32
F32R = mybir.dt.float32r
I32 = mybir.dt.int32
ALU = mybir.AluOpType
ACT = mybir.ActivationFunctionType
AX = mybir.AxisListType

P = 128
T = 256
TT = T // P
D = 2048
KC = D // P
CB = 4
NB = CB * P
UK = 2
UE = UK * NB
RING = 4
MLA_H, NOPE, ROPE, Q_LAT, KV_LAT = 8, 128, 64, 512, 256
DIFF_H = 4
X_H = 4
A_H = R_H = 8
HID = 5632
PLE = 256
GROUPS = (4, 4, 3)
assert sum(GROUPS) * NB == HID and max(GROUPS) * CB <= KC
LAMBDA_INIT = 0.8 - 0.6 * 1.0
EPS = 1e-6
EPS_DIFF = 1e-5
NEG = -1e30
BCOLS = CB * T

VECTORS = (("g_mix", KC), ("g_q_lat", Q_LAT // P), ("g_kv_lat", KV_LAT // P), ("g_xattn", KC), ("g_mem", KC),
           ("g_ffn", KC), ("g_final", KC), ("g_mix_2", KC), ("g_ffn_2", KC), ("g_ple_2", KC),
           ("b_ple_gate_2", KC), ("g_ret_2", R_H), ("g_diff_sub", 2), ("q_norm_2", 1), ("k_norm_2", 1),
           ("lambda_q1", 1), ("lambda_q2", 1), ("lambda_k1", 1), ("lambda_k2", 1))
VCOL = {}
for _name, _n in VECTORS:
    VCOL[_name] = sum(n for m, n in VECTORS[:len(VCOL)])
VN = sum(n for _, n in VECTORS)
VCOL["g_both"] = VN

THETA = 10000.0
ROUNDER = 1.5 * 2.0 ** 23
TWO_PI_1 = 6.28125
TWO_PI_2 = round((2 * np.pi - TWO_PI_1) * 2 ** 20) / 2 ** 20
TWO_PI_PARTS = (TWO_PI_1, TWO_PI_2, float(2 * np.pi - TWO_PI_1 - TWO_PI_2))
PI_IN = 3.1415925

C_IDENT, C_MASK, C_FREQ, C_N = 0, P, 2 * P, 2 * P + 4

U_IN = (Q_LAT + 512 + 3 * 1024) // NB * (KC // UK)
U_UQ = 3 * (Q_LAT // P // UK)
U_UKV = 4 * (KV_LAT // P // UK)
U_X = KC // UK
U_RES = D // NB * (KC // UK)
U_XO = D // NB * (CB // UK)
U_MLP = 2 * sum(GROUPS) * (KC // UK) + sum(D // NB * g * CB // UK for g in GROUPS)
U_IN2 = 14 * (KC // UK)
U_PLE = D // NB * (PLE // P // UK)
UNITS = U_IN + U_UQ + U_UKV + 2 * U_X + U_RES + U_X + U_XO + U_MLP + U_IN2 + U_RES + U_MLP + U_PLE + U_RES
AT_MEM = U_IN + U_UQ + U_UKV + RING
AT_DECAY = AT_MEM - RING + 2 * U_X + U_RES + U_X + U_XO + U_MLP + U_IN2 + RING
AT_P = AT_DECAY - RING + U_RES + U_MLP + RING
N_MEM, N_DECAY, N_P = D * T // P // UE, R_H // 2, 1
RAWS = UNITS + N_MEM + N_DECAY + N_P


class Tally:

    def __init__(self):
        self.fixed, self.per, self.turn = 0, 0, None

    def add(self, n=1):
        self.fixed += n
        return self.value()

    def value(self, back=0):
        if self.turn is None:
            return self.fixed - back
        return self.turn * self.per + (self.fixed - back)


@contextmanager
def turns(engine, n, counts):
    start = {tally: tally.fixed for tally in counts}
    with engine.Fori(0, n) as turn:
        for tally, per in counts.items():
            tally.turn, tally.per = turn, per
        yield turn
    for tally, per in counts.items():
        assert tally.fixed - start[tally] == per, (tally.fixed - start[tally], per)
        tally.fixed += (n - 1) * per
        tally.turn = None


FIRST_JOBS = [("diff", h) for h in range(DIFF_H)] + [("mla", h) for h in range(MLA_H)]
CROSS_JOBS = [("cross", h) for h in range(X_H)]
SECOND_JOBS = [("ret", h) for h in range(R_H)] + [("moba", h) for h in range(A_H)]
JOBS = FIRST_JOBS + CROSS_JOBS + SECOND_JOBS
SCALE = {"mla": (NOPE + ROPE) ** -0.5, "diff": P ** -0.5, "cross": P ** -0.5, "moba": P ** -0.5}


def nth(n, kinds):
    return sum(kind in kinds for kind, _ in JOBS[:n + 1])


SOFT = ("diff", "mla", "cross", "moba")
KEPT = ("diff", "ret")
SPLIT = ("mla", "cross", "moba")


def outputs_at(n0, n_jobs, step):
    return [n for n in range(n0, n0 + n_jobs) if n - n0 + (1 if JOBS[n][0] == "ret" else 3) == step]


def two_blocks(nc: bass.Bass, stream, x_in, vectors, consts, tables, positions, out):
    with ExitStack() as ctx:
        def sb(name, shape, dt=F32):
            return ctx.enter_context(nc.sbuf_tensor(name, shape, dt))

        def sem(name):
            return ctx.enter_context(nc.semaphore(name))

        raw = sb("raw", [P, RING, UE])
        w_hi = sb("w_hi", [P, RING, UE], F32R)
        w_lo = sb("w_lo", [P, RING, UE], F32R)
        x = sb("x", [P, KC * T])
        norm_hi = sb("norm_hi", [P, KC * T], F32R)
        norm_lo = sb("norm_lo", [P, KC * T], F32R)
        mix_hi = sb("mix_hi", [P, KC * T], F32R)
        mix_lo = sb("mix_lo", [P, KC * T], F32R)
        heads = sb("heads", [P, 14 * BCOLS])
        tmp_a = sb("tmp_a", [P, BCOLS])
        tmp_b = sb("tmp_b", [P, BCOLS])
        tmp_c = sb("tmp_c", [P, BCOLS])
        tmp_d = sb("tmp_d", [P, BCOLS])
        tab = sb("tab", [P, 4 * T])
        vec = sb("vec", [P, VN + KC])
        con = sb("con", [P, C_N])
        ones = sb("ones", [P, P])
        r_main = sb("r_main", [P, T + TT])
        r_aux = heads[:, 54 * T:55 * T + TT]
        r_kv = tmp_d[:, 0:T + TT]
        lam = sb("lam", [P, 4])
        nmax = sb("nmax", [P, 3, 4])
        rowsum = sb("rowsum", [P, 3, 4])

        acc = ctx.enter_context(nc.psum_tensor("acc", [P, 2, BCOLS], F32))
        pt = ctx.enter_context(nc.psum_tensor("pt", [P, 2, 2 * T], F32))
        po = ctx.enter_context(nc.psum_tensor("po", [P, 2, 2 * T], F32))

        raw_landed = [sem(f"raw_landed{i}") for i in range(RING)]
        x_landed = [sem(f"x_landed{i}") for i in range(D // NB)]
        vec_landed = sem("vec_landed")
        pos_landed = sem("pos_landed")
        tab_landed = sem("tab_landed")
        out_stored = sem("out_stored")
        w_hi_ready = sem("w_hi_ready")
        raw_read = sem("raw_read")
        w_used = sem("w_used")
        block_taken = sem("block_taken")
        rows_ready = sem("rows_ready")
        squares_ready = sem("squares_ready")
        tile_squares = sem("tile_squares")
        sums_ready = sem("sums_ready")
        sums_done = sem("sums_done")
        ms_ready = sem("ms_ready")
        root_ready = sem("root_ready")
        hi_ready = sem("hi_ready")
        kept_hi_ready = sem("kept_hi_ready")
        operand_ready = sem("operand_ready")
        swap_ready = sem("swap_ready")
        func_ready = sem("func_ready")
        heads_ready = sem("heads_ready")
        scores_done = sem("scores_done")
        nmax_ready = sem("nmax_ready")
        exp_ready = sem("exp_ready")
        probs_ready = sem("probs_ready")
        trans_done = sem("trans_done")
        probsT_ready = sem("probsT_ready")
        decayed_ready = sem("decayed_ready")
        head_done = sem("head_done")
        kept_ready = sem("kept_ready")
        head_split = sem("head_split")
        lam_ready = sem("lam_ready")
        out_ready = sem("out_ready")
        act_done = sem("act_done")
        dve_done = sem("dve_done")

        def chunks(t, first, n=CB):
            return t[:, first * T:(first + n) * T]

        def block_of(t, b):
            return t[:, bass.ds(b * BCOLS, BCOLS)]

        def by_chunk(ap):
            return ap.rearrange("p (c t) -> p c t", c=CB)

        def over_chunks(row):
            return row.rearrange("p (o t) -> p o t", o=1).broadcast_to([P, CB, T])

        def gain(name, c):
            return vec[:, bass.ds(c + VCOL[name], 1)]

        ident = con[:, C_IDENT:C_IDENT + P]
        mask = con[:, C_MASK:C_MASK + P]
        cos_w, sin_w = tab[:, 0:T], tab[:, T:2 * T]
        cos_n, sin_n = tab[:, 2 * T:3 * T], tab[:, 3 * T:4 * T]
        probs = (tmp_a, tmp_b, tmp_d)
        both_pt = pt[:, :, :].rearrange("p a b -> p (a b)")

        DQ, DK, DV, QN, QR, KN, MV, KR = 0, 8, 16, 24, 32, 36, 44, 52
        XK, XV, XQ = 0, 4, 8
        AQ, AK, AV, RQ, RK, RV, RG = 0, 8, 16, 24, 32, 40, 48
        PP = 0
        NU = KC // UK
        NBD = D // NB
        ROTATED_FIRST, ROTATED_SECOND = 6, 8 + 2

        block = ctx.enter_context(nc.Block())

        @block.sync
        def _(sp):
            def load(r, slot):
                sp.dma_start(raw[:, slot, :], stream[bass.ds(r, 1)].rearrange("o p n -> (o p) n"))\
                    .then_inc(raw_landed[slot], 16)

            for b in range(NBD):
                sp.dma_start(block_of(x, b), block_of(x_in, b)).then_inc(x_landed[b], 16)
                load(b, b)
            with sp.Fori(0, RAWS // RING - 1) as i:
                for s in range(RING):
                    sp.wait_ge(raw_read, i * RING + (s + 1))
                    load(i * RING + (RING + s), s)
            for r in range(RAWS // RING * RING, RAWS):
                sp.wait_ge(raw_read, r - RING + 1)
                load(r, r % RING)
            for b in range(NBD):
                sp.wait_ge(out_ready, b + 1)
                sp.dma_start(block_of(out, b), block_of(x, b)).then_inc(out_stored, 16)
            sp.wait_ge(out_stored, 16 * NBD)

        @block.gpsimd
        def _(pool):
            pool.dma_start(vec[:, 0:VN], vectors).then_inc(vec_landed, 16)
            pool.dma_start(con[:, :], consts).then_inc(vec_landed, 16)
            pool.dma_start(tmp_b[:, 0:T].bitcast(I32), positions.rearrange("(o t) -> o t", o=1).broadcast_to([P, T]))\
                .then_inc(pos_landed, 16)
            pool.wait_ge(heads_ready, ROTATED_FIRST)
            pool.dma_start(tab[:, :], tables).then_inc(tab_landed, 16)

        @block.tensor
        def _(pe):
            units, blocks, operands, seen, tiles, means, rotated = (Tally() for _ in range(7))
            job = [0]
            norm, mix = (norm_hi, norm_lo), (mix_hi, mix_lo)

            def unit_split():
                u = units.fixed - 1
                extra = (u >= AT_MEM) * N_MEM + (u >= AT_DECAY) * N_DECAY + (u >= AT_P) * N_P
                return units.value() + extra

            def one_block(n_units, act, k0=0, token_major=False, need=None, mid=None, mid_at=5):
                act_hi, act_lo = act
                blocks.add()
                slot = (blocks.fixed - 1) % 2
                if blocks.fixed > 2:
                    pe.wait_ge(block_taken, blocks.value(2))
                for ki in range(n_units):
                    units.add()
                    s = (units.fixed - 1) % RING
                    pe.wait_ge(raw_read, unit_split())
                    if need:
                        pe.wait_ge(*need(ki))
                    for c in range(TT if token_major else CB):
                        for kk in range(UK):
                            k = k0 + ki * UK + kk
                            clear = ki == 0 and kk == 0 and (token_major or c % 2 == 0)
                            if token_major:
                                order = ((w_hi, act_hi), (w_lo, act_hi), (w_hi, act_lo))
                            else:
                                order = ((w_hi, act_hi), (w_hi, act_lo), (w_lo, act_hi))
                            for i, (w, a) in enumerate(order):
                                if token_major:
                                    last = pe.matmul(acc[:, slot, c * NB:(c + 1) * NB],
                                                     a[:, k * T + c * P:k * T + (c + 1) * P],
                                                     w[:, s, kk * NB:(kk + 1) * NB], start=clear and i == 0,
                                                     stop=ki == n_units - 1, skip_group_check=True)
                                else:
                                    last = pe.matmul(acc[:, slot, c * T:(c + 1) * T],
                                                     w[:, s, kk * NB + c * P:kk * NB + (c + 1) * P],
                                                     a[:, k * T:(k + 1) * T], start=clear and i == 0,
                                                     stop=ki == n_units - 1, skip_group_check=True)
                    last.then_inc(w_used, 1)
                    if mid and ki == mid_at:
                        mid()

            def released(n):
                if n >= 0:
                    kind = JOBS[n][0]
                    if kind in KEPT:
                        pe.wait_ge(kept_ready, nth(n, KEPT))
                    else:
                        pe.wait_ge(head_split, nth(n, SPLIT))

            def means_read():
                if means.fixed:
                    pe.wait_ge(ms_ready, means.fixed)

            def token_sums(src, n, ready=None, bank=0, both=False):
                if bank == 0:
                    means_read()
                released(job[0] - 1)
                released(job[0] - 2)
                if ready:
                    pe.wait_ge(*ready)
                for c in range(n):
                    last = pe.matmul(po[:, bank, 0:T], ones[:, :], src[:, c * T:(c + 1) * T],
                              start=c == 0, stop=c == n - 1, skip_group_check=True)
                for t in range(TT if both else 0):
                    for c in range(n):
                        last = pe.matmul(po[:, bank, T + t:T + t + 1], src[:, c * T + t * P:c * T + (t + 1) * P],
                                         ones[:, 0:1], start=False, stop=c == n - 1, skip_group_check=True)
                last.then_inc(sums_done, 1)
                means.add()

            def added_sums(both=False):
                return lambda: token_sums(tmp_c, CB, (sums_ready, seen.add(NBD)), both=both)

            def tile_sums(n, both=False):
                return lambda: token_sums(tmp_c, n, (tile_squares, tiles.add()), both=both)

            def head_sums(src, per=1):
                pe.wait_ge(tile_squares, tiles.add())
                means_read()
                if job[0]:
                    pe.wait_ge(probsT_ready, nth(transposed[0], SOFT))
                for h in range(4):
                    for c in range(per):
                        last = pe.matmul(pt[:, h // 2, h % 2 * T:(h % 2 + 1) * T], ones[:, :],
                                         src[:, (h * per + c) * T:(h * per + c + 1) * T],
                                         start=c == 0 and h % 2 == 0, stop=c == per - 1, skip_group_check=True)
                last.then_inc(sums_done, 1)
                means.add()

            transposed = [-1]

            def operand_need(base):
                return lambda ki: (operand_ready, base + ki * UK // CB + 1)

            def residual(n_units, act, need=None, mid=None, peel=False):
                if mid or peel:
                    one_block(n_units, act, need=need, mid=mid)
                    one_block(n_units, act)
                with turns(pe, NBD // 2 - bool(mid or peel), {units: 2 * n_units, blocks: 2}):
                    for _ in range(2):
                        one_block(n_units, act, need=None if mid or peel else need)

            def mlp(need):
                for g, n in enumerate(GROUPS):
                    if g == 0:
                        one_block(NU, norm, need=need, mid=added_sums())
                        one_block(NU, norm)
                    with turns(pe, n - (g == 0), {units: 2 * NU, blocks: 2}):
                        one_block(NU, norm)
                        one_block(NU, norm)
                    down = operand_need(operands.fixed)
                    operands.add(n)
                    nd = n * CB // UK
                    with turns(pe, NBD // 2, {units: 2 * nd, blocks: 2}):
                        for _ in range(2):
                            one_block(nd, mix, need=down)

            def scores(n):
                kind, h = JOBS[n]
                slot = n % 2
                if n >= 2:
                    if JOBS[n - 2][0] == "ret":
                        pe.wait_ge(decayed_ready, nth(n - 2, ("ret",)))
                    else:
                        pe.wait_ge(exp_ready, nth(n - 2, SOFT))
                if kind == "ret":
                    for kk in range(TT):
                        last = pe.matmul(acc[:, slot, kk * (T + P):(kk + 1) * T],
                                         heads[:, (RK + h) * T + kk * P:(RK + h) * T + (kk + 1) * P],
                                         heads[:, (RQ + h) * T + kk * P:(RQ + h + 1) * T],
                                         start=kk == 0, stop=True, skip_group_check=True)
                    last.then_inc(scores_done, 1)
                    return
                for comp in range(2 if kind == "diff" else 1):
                    parts = {"diff": [(DQ + 2 * h + comp, DK + 2 * h + comp)],
                             "mla": [(QN + h, KN + h), (QR + h // 2, KR + h % 2)],
                             "cross": [(XQ + h, XK + h)], "moba": [(AQ + h, AK + h)]}[kind]
                    for t in range(TT):
                        width = (t + 1) * P if kind == "moba" else T
                        for i, (q, k) in enumerate(parts):
                            at = (comp * TT + t) * T
                            last = pe.matmul(acc[:, slot, at:at + width],
                                             heads[:, q * T + t * P:q * T + (t + 1) * P],
                                             heads[:, k * T:k * T + width], start=t == 0 and i == 0,
                                             stop=i == len(parts) - 1, skip_group_check=True)
                last.then_inc(scores_done, 1)

            def transposes(n):
                kind, h = JOBS[n]
                if kind == "ret":
                    return
                pe.wait_ge(probs_ready, nth(n, SOFT))
                if n >= 2 and nth(n - 2, SOFT):
                    pe.wait_ge(probsT_ready, nth(n - 2, SOFT))
                means_read()
                prob = probs[n % 3]
                for kk in range(TT):
                    for t in range(kk if kind == "moba" else 0, TT):
                        last = pe.transpose(pt[:, n % 2, kk * T + t * P:kk * T + (t + 1) * P],
                                            prob[:, t * T + kk * P:t * T + (kk + 1) * P], ident)
                last.then_inc(trans_done, 1)
                transposed[0] = n

            def values(n):
                kind, h = JOBS[n]
                if kind == "ret":
                    pe.wait_ge(decayed_ready, nth(n, ("ret",)))
                else:
                    pe.wait_ge(probsT_ready, nth(n, SOFT))
                released(n - 2)
                means_read()
                prob_t = tmp_c[:, n % 2 * 2 * T:(n % 2 + 1) * 2 * T]
                first, width, wide = {"diff": (DV, 8 * P, 2), "mla": (MV, 8 * P, 1), "cross": (XV, 4 * P, 1),
                                      "ret": (RV, 8 * P, 1), "moba": (AV, 8 * P, 1)}[kind]
                for e in range(wide):
                    for kk in range(TT):
                        q0 = kk * P if kind in ("ret", "moba") else 0
                        v = first * T + kk * width + (h * wide + e) * P
                        last = pe.matmul(po[:, n % 2, e * T + q0:(e + 1) * T], heads[:, v:v + P],
                                         prob_t[:, kk * T + q0:(kk + 1) * T], start=kk == 0 and e == 0,
                                         stop=kk == TT - 1, skip_group_check=True)
                last.then_inc(head_done, 1)
                job[0] = n + 1

            def attend(n_jobs, at=None):
                n0 = job[0]
                pe.wait_ge(block_taken, blocks.fixed)
                if rotated.fixed:
                    pe.wait_ge(heads_ready, rotated.fixed)
                for i in range(n_jobs + 3):
                    if i < n_jobs:
                        scores(n0 + i)
                    if at and i in at:
                        at[i]()
                    if 2 <= i < n_jobs + 2:
                        transposes(n0 + i - 2)
                    for n in outputs_at(n0, n_jobs, i):
                        values(n)

            pe.wait_ge(vec_landed, 32)
            pe.wait_ge(lam_ready, 1)
            pe.matmul(po[:, 1, 0:2], ones[:, :], lam[:, 0:2], start=True, stop=True).then_inc(sums_done, 1)

            one_block(NU, norm, need=operand_need(0), mid=added_sums(True), mid_at=6)
            one_block(NU, norm, mid=tile_sums(Q_LAT // P))
            one_block(NU, norm, mid=tile_sums(KV_LAT // P, True))
            one_block(NU, norm)
            one_block(NU, norm)
            one_block(NU, norm)
            one_block(NU, norm, token_major=True)
            one_block(NU, norm, token_major=True)
            operands.add(NBD + 2)
            for _ in range(3):
                one_block(Q_LAT // P // UK, mix, need=lambda ki: (operand_ready, NBD + 2))
            for i in range(4):
                one_block(1, mix, k0=CB, token_major=i >= 2)
            rotated.add(ROTATED_FIRST)
            attend(len(FIRST_JOBS), {7: lambda: head_sums(chunks(heads, DK, 8), 2)})

            one_block(NU, norm, need=lambda ki: (raw_read, AT_MEM + ki * UK // CB + 1), mid=added_sums(True),
                      mid_at=6)
            one_block(NU, norm, token_major=True)
            operands.add(1)
            pe.wait_ge(operand_ready, operands.fixed)
            pe.wait_ge(head_split, MLA_H)
            residual(NU, mix)
            one_block(NU, norm, need=operand_need(operands.fixed), mid=added_sums(), mid_at=6)
            operands.add(NBD)
            attend(len(CROSS_JOBS))
            residual(CB // UK, mix, need=lambda ki: (head_split, MLA_H + UK * (ki + 1)))
            need = operand_need(operands.fixed)
            operands.add(NBD)
            mlp(need)

            def both_sums():
                token_sums(tmp_c, CB, (sums_ready, seen.add(2 * NBD)), both=True)
                token_sums(tmp_b, CB, bank=1, both=True)

            one_block(NU, norm, need=operand_need(operands.fixed), mid=both_sums, mid_at=6)
            operands.add(NBD)
            for b in range(1, 5):
                one_block(NU, norm, token_major=b == 4, mid=lambda: head_sums(tmp_b), mid_at=2)
            one_block(NU, norm, token_major=True)
            with turns(pe, 2, {units: 2 * NU, blocks: 2}):
                one_block(NU, norm)
                one_block(NU, norm)
            for b in range(4):
                one_block(NU, norm, token_major=b < 2)
            rotated.add(ROTATED_SECOND)
            attend(len(SECOND_JOBS), {5: lambda: head_sums(chunks(heads, RK)),
                                      9: lambda: head_sums(chunks(heads, RK + 4))})
            operands.add(2)
            pe.wait_ge(operand_ready, operands.fixed)
            pe.wait_ge(head_split, nth(len(JOBS), SPLIT))
            residual(NU, mix, peel=True)
            need = operand_need(operands.fixed)
            operands.add(NBD)
            mlp(need)

            for _ in range(NBD):
                one_block(1, mix, need=lambda ki: (raw_read, AT_P + N_MEM + N_DECAY + N_P))
            residual(NU, norm, need=operand_need(operands.fixed), mid=added_sums())
            assert units.fixed == UNITS

        @block.scalar
        def _(act):
            raws, units, taken, rows, means, nmaxs = (Tally() for _ in range(6))
            job = [0]

            def take_raw():
                raws.add()
                at = raws.fixed - 1
                turn = at // RING + 1
                if raws.turn is not None:
                    turn = raws.turn * (raws.per // RING) + turn
                act.wait_ge(raw_landed[at % RING], turn * 16)
                return raw[:, at % RING, :]

            def split(n):
                for _ in range(n):
                    if units.turn is None and units.fixed == UNITS:
                        return
                    src = take_raw()
                    units.add()
                    if units.fixed > RING:
                        act.wait_ge(w_used, units.value(RING))
                    act.activation(w_hi[:, (units.fixed - 1) % RING, :], src, ACT.Copy).then_inc(w_hi_ready, 1)

            def roots(r):
                act.wait_ge(ms_ready, means.add())
                act.activation(r, r, ACT.Sqrt).then_inc(root_ready, 1)

            def wait_taken(n=1):
                act.wait_ge(block_taken, taken.add(n))

            def wait_rows():
                act.wait_ge(rows_ready, rows.add())

            def hi_gained(src, dst, b, name, n=CB):
                for c in range(n):
                    last = act.activation(dst[:, bass.ds(b * BCOLS + c * T, T)], src[:, c * T:(c + 1) * T], ACT.Copy,
                                          scale=gain(name, b * CB + c))
                last.then_inc(hi_ready, 1)

            def squares(src):
                act.activation(tmp_a[:, :], src, ACT.Square).then_inc(squares_ready, 1)

            def swap(half):
                for a in range(0, P, 2 * half):
                    act.activation(tmp_b[a:a + half, :], tmp_a[a + half:a + 2 * half, :], ACT.Copy)
                    last = act.activation(tmp_b[a + half:a + 2 * half, :], tmp_a[a:a + half, :], ACT.Copy)
                last.then_inc(swap_ready, 1)

            def residual_block(b, name):
                wait_taken()
                squares(block_of(x, b))
                hi_gained(block_of(x, b), norm_hi, b, name)

            def residual(n_units, name, peel=0):
                for b in range(peel):
                    split(n_units)
                    residual_block(b, name)
                with turns(act, (NBD - peel) // 2, {units: 2 * n_units, raws: 2 * n_units, taken: 2}) as i:
                    for j in range(2):
                        split(n_units)
                        residual_block(i * 2 + (j + peel), name)

            def mlp(last_gain):
                def pair(i, first=False):
                    split(NU)
                    if first:
                        roots(r_main[:, 0:T])
                    wait_taken()
                    act.activation(tmp_b[:, :], tmp_a[:, :], ACT.Sigmoid).then_inc(func_ready, 1)
                    split(NU)
                    taken.add()
                    wait_rows()
                    act.activation(block_of(mix_hi, i), tmp_b[:, :], ACT.Copy).then_inc(hi_ready, 1)

                for g, n in enumerate(GROUPS):
                    nd = n * CB // UK
                    first = int(g == 0)
                    if first:
                        pair(0, True)
                    with turns(act, n - first, {units: 2 * NU, raws: 2 * NU, taken: 2, rows: 1}) as i:
                        pair(i + first)
                    if g < len(GROUPS) - 1:
                        with turns(act, NBD // 2, {units: 2 * nd, raws: 2 * nd, taken: 2}):
                            split(2 * nd)
                            taken.add(2)
                    elif last_gain:
                        residual(nd, last_gain)
                    else:
                        for b in range(NBD):
                            split(nd)
                            wait_taken()
                            squares(block_of(x, b))
                            for c in range(CB):
                                last = act.activation(chunks(tmp_d, c, 1), chunks(x, b * CB + c, 1), ACT.Square,
                                                      scale=gain("g_final", b * CB + c))
                            last.then_inc(squares_ready, 1)
                            hi_gained(block_of(x, b), norm_hi, b, "g_both")

            def exps(n):
                kind, h = JOBS[n]
                if kind == "ret":
                    return
                if n >= 3 and JOBS[n - 3][0] in SOFT:
                    act.wait_ge(trans_done, nth(n - 3, SOFT))
                act.wait_ge(nmax_ready, nth(n, SOFT))
                prob = probs[n % 3]
                for i in range(2 * TT if kind == "diff" else TT):
                    width = (i + 1) * P if kind == "moba" else T
                    last = act.activation(prob[:, i * T:i * T + width], acc[:, n % 2, i * T:i * T + width], ACT.Exp,
                                          bias=nmax[:, n % 3, i:i + 1], scale=SCALE[kind],
                                          accum_out=rowsum[:, n % 3, i:i + 1])
                last.then_inc(exp_ready, 1)

            def copy_transposed(n):
                kind, h = JOBS[n]
                if kind == "ret":
                    return
                act.wait_ge(trans_done, nth(n, SOFT))
                if n >= 2:
                    act.wait_ge(head_done, n - 1)
                dst = tmp_c[:, n % 2 * 2 * T:(n % 2 + 1) * 2 * T]
                if kind == "moba":
                    act.activation(dst[:, 0:T], pt[:, n % 2, 0:T], ACT.Copy)
                    last = act.activation(dst[:, T + P:], pt[:, n % 2, T + P:], ACT.Copy)
                else:
                    last = act.activation(dst, pt[:, n % 2, :], ACT.Copy)
                last.then_inc(probsT_ready, 1)

            def keep(n):
                kind, h = JOBS[n]
                act.wait_ge(head_done, n + 1)
                if kind == "diff":
                    act.activation(chunks(heads, DQ + 2 * h, 2), po[:, n % 2, :], ACT.Copy).then_inc(kept_ready, 1)
                elif kind == "ret":
                    act.activation(chunks(heads, RQ + h, 1), po[:, n % 2, 0:T], ACT.Copy).then_inc(kept_ready, 1)
                else:
                    act.activation(chunks(mix_hi, h, 1), po[:, n % 2, 0:T], ACT.Copy).then_inc(hi_ready, 1)

            def attend(n_jobs, at=None):
                n0 = job[0]
                for i in range(n_jobs + 3):
                    if 2 <= i < n_jobs + 2:
                        copy_transposed(n0 + i - 2)
                    if i < n_jobs:
                        exps(n0 + i)
                    for n in outputs_at(n0, n_jobs, i):
                        keep(n)
                    if at and i in at:
                        at[i]()
                job[0] += n_jobs

            def head_squares(src, dst, kept):
                act.wait_ge(kept_ready, kept)
                act.activation(dst, src, ACT.Square).then_inc(tile_squares, 1)

            def head_hi(first, src):
                wait_rows()
                act.activation(chunks(mix_hi, first, src.shape[1] // T), src, ACT.Copy).then_inc(kept_hi_ready, 1)

            act.wait_ge(vec_landed, 32)
            for b in range(NBD):
                act.wait_ge(x_landed[b], 16)
                hi_gained(block_of(x, b), norm_hi, b, "g_mix")
                split(1)
                if b:
                    act.wait_ge(sums_ready, b)
                squares(block_of(x, b))
            wait_rows()
            act.activation(lam[:, 2:4], lam[:, 2:4], ACT.Exp).then_inc(func_ready, 1)

            split(4)
            wait_rows()
            act.activation(tab[:, :], tab[:, :], ACT.Sin).then_inc(func_ready, 1)
            split(NU - 4)
            roots(r_main[:, :])
            wait_taken()
            act.activation(tmp_c[:, :], tmp_a[:, :], ACT.Square).then_inc(tile_squares, 1)
            hi_gained(tmp_a, mix_hi, 0, "g_q_lat")
            split(NU)
            roots(r_aux[:, 0:T])
            wait_taken()
            act.activation(tmp_c[:, 0:2 * T], tmp_a[:, 0:2 * T], ACT.Square).then_inc(tile_squares, 1)
            for c in range(KV_LAT // P):
                last = act.activation(chunks(mix_hi, CB + c, 1), chunks(tmp_a, c, 1), ACT.Copy,
                                      scale=gain("g_kv_lat", c))
            last.then_inc(hi_ready, 1)
            split(NU)
            roots(r_kv[:, :])
            wait_taken()
            swap(P // 2)
            for _ in range(3):
                split(NU)
                wait_taken()
                swap(P // 2)
            split(2 * NU + 4)
            taken.add(4)
            split(2)
            wait_taken()
            swap(ROPE // 2)
            split(4)
            taken.add(4)
            attend(len(FIRST_JOBS), {
                6: lambda: head_squares(chunks(heads, DQ, 8), chunks(heads, DK, 8), DIFF_H),
                7: lambda: roots(chunks(heads, DV)),
                9: lambda: head_hi(8, chunks(heads, DQ, 8))})

            for m in range(N_MEM):
                src = take_raw()
                wait_rows()
                squares(src)
                hi_gained(src, norm_hi, m, "g_mem")
            split(NU)
            roots(r_aux[:, :])
            taken.add(2)
            split(NU)
            residual(NU, "g_xattn")
            split(NU)
            roots(r_main[:, 0:T])
            taken.add()
            attend(len(CROSS_JOBS))
            residual(CB // UK, "g_ffn")
            mlp(None)

            split(NU)
            roots(r_aux[:, :])
            means.add()
            wait_rows()
            act.activation(r_main[:, :], r_main[:, :], ACT.Sqrt).then_inc(root_ready, 1)
            for b in range(4):
                wait_taken()
                act.activation(tmp_b[:, :], tmp_a[:, :], ACT.Square).then_inc(tile_squares, 1)
                split(4)
                roots(tmp_b[:, :])
                split(2)
                wait_rows()
                swap(P // 2)
                split(2)
            taken.add(2)
            split(NU)
            with turns(act, 4, {units: NU, raws: NU, taken: 1}):
                split(NU)
                wait_taken()
                swap(P // 2)
            taken.add(2)
            split(2 * NU)
            for b in range(2):
                split(NU)
                wait_taken()
                act.activation(tmp_b[:, :], tmp_a[:, :], ACT.Sigmoid).then_inc(func_ready, 1)
            raws.add(N_DECAY)
            ret_kept = DIFF_H + 4
            attend(len(SECOND_JOBS), {
                4: lambda: head_squares(chunks(heads, RQ), chunks(heads, RK), ret_kept),
                5: lambda: roots(chunks(heads, RK)),
                7: lambda: head_hi(8, chunks(heads, RQ)),
                8: lambda: head_squares(chunks(heads, RQ + 4), chunks(heads, RK + 4), ret_kept + 4),
                9: lambda: roots(chunks(heads, RK + 4)),
                11: lambda: head_hi(12, chunks(heads, RQ + 4))})
            residual(NU, "g_ffn_2")
            mlp("g_ple_2")

            src = take_raw()
            act.activation(mix_hi[:, 0:2 * T], src[:, 0:2 * T], ACT.Copy).then_inc(hi_ready, 1)
            split(NBD)
            taken.add(NBD)
            for b in range(NBD):
                split(NU)
                if b == 0:
                    roots(r_main[:, 0:T])
                wait_taken()
                for c in range(CB):
                    last = act.activation(chunks(tmp_b, c, 1), chunks(tmp_a, c, 1), ACT.Sigmoid,
                                          bias=gain("b_ple_gate_2", b * CB + c))
                last.then_inc(func_ready, 1)
            assert units.fixed == UNITS and raws.fixed == RAWS

        @block.vector
        def _(dve):
            (raws, units, ends, taken, his, squared, added, sums, roots_n, swaps, funcs, rows, own,
             kept_his) = (Tally() for _ in range(14))
            job = [0]

            def link(ins):
                ins.then_inc(dve_done, 1)
                dve.wait_ge(dve_done, own.add())

            def next_raw():
                raws.add()
                return raw[:, (raws.fixed - 1) % RING, :]

            def split(n):
                for _ in range(n):
                    if units.turn is None and units.fixed == UNITS:
                        return
                    src = next_raw()
                    dve.wait_ge(w_hi_ready, units.add())
                    s = (units.fixed - 1) % RING
                    dve.tensor_tensor(w_lo[:, s, :], src, w_hi[:, s, :].bitcast(F32), ALU.subtract)\
                        .then_inc(raw_read, 1)

            def block_end(n_units):
                dve.wait_ge(w_used, ends.add(n_units))
                taken.add()
                return acc[:, (taken.fixed - 1) % 2, :]

            def took(ins):
                ins.then_inc(block_taken, 1)
                dve.wait_ge(block_taken, taken.value())

            def take_scaled(n_units, dst, r):
                src = block_end(n_units)
                took(dve.tensor_tensor(by_chunk(dst), by_chunk(src), over_chunks(r[:, 0:T]), ALU.mult))

            def take_token_major(n_units, first, width, b, r):
                src = block_end(n_units)
                for t in range(TT):
                    at = first * T + t * width + b * NB
                    last = dve.tensor_scalar(heads[:, at:at + NB], src[:, t * NB:(t + 1) * NB],
                                             r[:, T + t:T + t + 1], None, ALU.mult)
                took(last)

            def take_added(n_units, b):
                src = block_end(n_units)
                took(dve.tensor_tensor(block_of(x, b), block_of(x, b), src, ALU.add))

            def root_ready_of(r):
                dve.wait_ge(root_ready, roots_n.add())
                link(dve.reciprocal(r, r))

            def mean_squares(r, src, count, eps):
                dve.wait_ge(sums_done, sums.add())
                dve.tensor_scalar(r, src, 1.0 / count, eps, ALU.mult, ALU.add).then_inc(ms_ready, 1)

            def token_norm(r, count, both=False):
                w = T + TT if both else T
                mean_squares(r[:, 0:w], po[:, 0, 0:w], count, EPS)
                root_ready_of(r[:, 0:w])

            def add_squares(src=tmp_a, dst=tmp_c):
                dve.wait_ge(squares_ready, squared.add())
                if added.fixed:
                    dve.wait_ge(sums_ready, added.value())
                dve.tensor_tensor(dst[:, :], dst[:, :], src[:, :], ALU.add).then_inc(sums_ready, 1)
                added.add()

            def low(dst, src, hi, done=operand_ready):
                dve.wait_ge(hi_ready, his.add())
                dve.tensor_tensor(dst, src, hi.bitcast(F32), ALU.subtract).then_inc(done, 1)

            def low_gained(src, dst, b, name, n=CB, first=0, done=operand_ready):
                dve.wait_ge(hi_ready, his.add())
                dst_hi, dst_lo = dst
                for c in range(n):
                    at = bass.ds(b * BCOLS + (first + c) * T, T)
                    last = dve.scalar_tensor_tensor(out=dst_lo[:, at], in0=src[:, c * T:(c + 1) * T],
                                                    scalar=gain(name, b * CB + c), in1=dst_hi[:, at].bitcast(F32),
                                                    op0=ALU.mult, op1=ALU.subtract)
                last.then_inc(done, 1)

            def rotate(dst, cos, sin):
                dve.wait_ge(swap_ready, swaps.add())
                dve.tensor_tensor(by_chunk(dst), by_chunk(tmp_a[:, :]), over_chunks(cos), ALU.mult)
                link(dve.tensor_tensor(by_chunk(tmp_b[:, :]), by_chunk(tmp_b[:, :]), over_chunks(sin), ALU.mult))
                dve.tensor_tensor(dst, dst, tmp_b[:, :], ALU.add).then_inc(heads_ready, 1)

            def clear_sums(*which):
                for t in which:
                    link(dve.memset(t[:, :], 0.0))

            def residual_block(n_units, b, name):
                take_added(n_units, b)
                add_squares()
                low_gained(block_of(x, b), (norm_hi, norm_lo), b, name)

            def residual(n_units, name):
                clear_sums(tmp_c)
                with turns(dve, NBD // 2, {units: 2 * n_units, raws: 2 * n_units, ends: 2 * n_units, taken: 2,
                                           squared: 2, added: 2, his: 2}) as i:
                    for j in range(2):
                        split(n_units)
                        residual_block(n_units, i * 2 + j, name)

            def mlp(last_gain):
                def pair(i, first=False):
                    split(NU)
                    if first:
                        token_norm(r_main, D)
                    take_scaled(NU, tmp_a[:, :], r_main)
                    split(NU)
                    dve.wait_ge(func_ready, funcs.add())
                    link(dve.tensor_tensor(tmp_a[:, :], tmp_a[:, :], tmp_b[:, :], ALU.mult))
                    take_scaled(NU, tmp_b[:, :], r_main)
                    dve.tensor_tensor(tmp_b[:, :], tmp_b[:, :], tmp_a[:, :], ALU.mult).then_inc(rows_ready, 1)
                    dve.wait_ge(rows_ready, rows.add())
                    low(block_of(mix_lo, i), tmp_b[:, :], block_of(mix_hi, i))

                for g, n in enumerate(GROUPS):
                    nd = n * CB // UK
                    first = int(g == 0)
                    if first:
                        pair(0, True)
                    with turns(dve, n - first, {units: 2 * NU, raws: 2 * NU, ends: 2 * NU, taken: 2, funcs: 1,
                                                own: 1, rows: 1, his: 1}) as i:
                        pair(i + first)
                    if g < len(GROUPS) - 1:
                        with turns(dve, NBD // 2, {units: 2 * nd, raws: 2 * nd, ends: 2 * nd, taken: 2}) as i:
                            for j in range(2):
                                split(nd)
                                take_added(nd, i * 2 + j)
                    elif last_gain:
                        residual(nd, last_gain)
                    else:
                        clear_sums(tmp_c, tmp_b)
                        with turns(dve, NBD // 2, {units: 2 * nd, raws: 2 * nd, ends: 2 * nd, taken: 2, squared: 4,
                                                   added: 4, his: 2}) as i:
                            for j in range(2):
                                split(nd)
                                b = i * 2 + j
                                take_added(nd, b)
                                add_squares()
                                add_squares(tmp_d, tmp_b)
                                low_gained(block_of(x, b), (norm_hi, norm_lo), b, "g_both")

            def maxima(n):
                kind, h = JOBS[n]
                dve.wait_ge(scores_done, n + 1)
                s = acc[:, n % 2, :]
                if kind == "ret":
                    if h % 2 == 0:
                        src = next_raw()
                        at = raws.fixed - 1
                        dve.wait_ge(raw_landed[at % RING], 16 * (at // RING + 1))
                        decay[0] = src
                    if n >= 2:
                        dve.wait_ge(head_done, n - 1)
                    dst = tmp_c[:, n % 2 * 2 * T:(n % 2 + 1) * 2 * T]
                    d = decay[0][:, h % 2 * 2 * T:(h % 2 + 1) * 2 * T]
                    dve.tensor_tensor(dst[:, 0:T], s[:, 0:T], d[:, 0:T], ALU.mult)
                    dve.tensor_tensor(dst[:, T + P:], s[:, T + P:2 * T], d[:, T + P:], ALU.mult)\
                        .then_inc(decayed_ready, 1)
                    if h == R_H - 1:
                        dve.wait_ge(decayed_ready, R_H)
                        dve.sem_inc(raw_read, N_DECAY)
                    return
                w = 2 * TT if kind == "diff" else TT
                m = nmax[:, n % 3, 0:w]
                if kind == "moba":
                    for t in range(TT):
                        diag = s[:, t * (T + P):t * (T + P) + P]
                        last = dve.tensor_tensor(diag, diag, mask, ALU.add)
                    link(last)
                    for t in range(TT):
                        last = dve.tensor_reduce(nmax[:, n % 3, t:t + 1], s[:, t * T:t * T + (t + 1) * P], AX.X, ALU.max)
                    link(last)
                else:
                    link(dve.tensor_reduce(m, s[:, 0:w * T].rearrange("p (i t) -> p i t", i=w), AX.X, ALU.max))
                dve.tensor_scalar(m, m, -SCALE[kind], None, ALU.mult).then_inc(nmax_ready, 1)

            decay = [None]

            def normalise(n):
                kind, h = JOBS[n]
                if kind == "ret":
                    return
                dve.wait_ge(exp_ready, nth(n, SOFT))
                prob = probs[n % 3]
                w = 2 * TT if kind == "diff" else TT
                sum_ = rowsum[:, n % 3, :]
                link(dve.reciprocal(sum_[:, 0:w], sum_[:, 0:w]))
                if kind == "diff":
                    link(dve.tensor_scalar(sum_[:, TT:w], sum_[:, TT:w], lam[:, 0:1], None, ALU.mult))
                    for t in range(TT):
                        p2 = chunks(prob, TT + t, 1)
                        last = dve.tensor_scalar(p2, p2, sum_[:, TT + t:TT + t + 1], None, ALU.mult)
                    link(last)
                    for t in range(TT):
                        last = dve.scalar_tensor_tensor(out=chunks(prob, t, 1), in0=chunks(prob, t, 1),
                                                        scalar=sum_[:, t:t + 1], in1=chunks(prob, TT + t, 1),
                                                        op0=ALU.mult, op1=ALU.add)
                else:
                    for t in range(TT):
                        p = prob[:, t * T:t * T + ((t + 1) * P if kind == "moba" else T)]
                        last = dve.tensor_scalar(p, p, sum_[:, t:t + 1], None, ALU.mult)
                last.then_inc(probs_ready, 1)

            def split_head(n):
                kind, h = JOBS[n]
                if kind in SPLIT:
                    low(chunks(mix_lo, h, 1), po[:, n % 2, 0:T], chunks(mix_hi, h, 1), head_split)

            def attend(n_jobs, at=None):
                n0 = job[0]
                for i in range(n_jobs + 4):
                    if i < n_jobs:
                        maxima(n0 + i)
                    if 1 <= i <= n_jobs:
                        normalise(n0 + i - 1)
                    for n in outputs_at(n0, n_jobs, i - 1):
                        split_head(n)
                    if at and i in at:
                        at[i]()
                job[0] += n_jobs

            def diff_scale():
                r = chunks(heads, DV)
                root_ready_of(r)
                link(dve.tensor_scalar(r, r, 1.0 - LAMBDA_INIT, None, ALU.mult))
                for e in range(2):
                    o = chunks(heads, DQ, 8).rearrange("p (h e t) -> p e h t", h=DIFF_H, e=2)[:, e]
                    last = dve.scalar_tensor_tensor(out=o, in0=o, scalar=gain("g_diff_sub", e), in1=by_chunk(r),
                                                    op0=ALU.mult, op1=ALU.mult)
                last.then_inc(rows_ready, 1)
                dve.wait_ge(rows_ready, rows.add())

            def ret_scale(half):
                r, o, g = chunks(heads, RK + 4 * half), chunks(heads, RQ + 4 * half), chunks(heads, RG + 4 * half)
                root_ready_of(r)
                for c in range(4):
                    last = dve.scalar_tensor_tensor(out=chunks(o, c, 1), in0=chunks(o, c, 1),
                                                    scalar=gain("g_ret_2", 4 * half + c), in1=chunks(r, c, 1),
                                                    op0=ALU.mult, op1=ALU.mult)
                link(last)
                dve.tensor_tensor(o, o, g, ALU.mult).then_inc(rows_ready, 1)
                dve.wait_ge(rows_ready, rows.add())

            def kept_low(first, src):
                n = src.shape[1] // T
                dve.wait_ge(kept_hi_ready, kept_his.add())
                dve.tensor_tensor(chunks(mix_lo, first, n), src, chunks(mix_hi, first, n).bitcast(F32), ALU.subtract)\
                    .then_inc(operand_ready, 1)

            dve.memset(ones[:, :], 1.0)
            dve.memset(chunks(heads, KR, 1)[P // 2:P, :], 0.0)
            dve.memset(chunks(heads, KR + 1, 1)[0:P // 2, :], 0.0)
            clear_sums(tmp_c)
            dve.wait_ge(vec_landed, 32)
            dve.tensor_tensor(lam[:, 0:2], vec[:, VCOL["lambda_q1"]:VCOL["lambda_q1"] + 2],
                              vec[:, VCOL["lambda_k1"]:VCOL["lambda_k1"] + 2], ALU.mult).then_inc(lam_ready, 1)
            link(dve.tensor_tensor(vec[:, VCOL["g_both"]:VCOL["g_both"] + KC], vec[:, VCOL["g_final"]:VCOL["g_final"] + KC],
                                   vec[:, VCOL["g_mix_2"]:VCOL["g_mix_2"] + KC], ALU.mult))
            for b in range(NBD):
                low_gained(block_of(x, b), (norm_hi, norm_lo), b, "g_mix")
                split(1)
                add_squares()
            dve.wait_ge(sums_done, sums.add())
            dve.tensor_copy(lam[:, 2:4], po[:, 1, 0:2]).then_inc(rows_ready, 1)
            dve.wait_ge(rows_ready, rows.add())

            dve.wait_ge(pos_landed, 16)
            pos, angle, turn_n = heads[:, 0:T], heads[:, BCOLS:2 * BCOLS], heads[:, 2 * BCOLS:3 * BCOLS]
            link(dve.tensor_copy(pos, tmp_b[:, 0:T].bitcast(I32)))
            for i in range(4):
                last = dve.tensor_scalar(chunks(angle, i, 1), pos, con[:, C_FREQ + i // 2:C_FREQ + i // 2 + 1], None,
                                         ALU.mult)
            link(last)
            dve.wait_ge(func_ready, funcs.add())
            link(dve.tensor_tensor(lam[:, 0:1], lam[:, 3:4], lam[:, 2:3], ALU.subtract))
            link(dve.tensor_scalar(lam[:, 0:1], lam[:, 0:1], -LAMBDA_INIT, None, ALU.add))
            split(2)
            for i in range(4):
                last = dve.tensor_scalar(chunks(turn_n, i, 1), chunks(angle, i, 1), 1.0 / (2 * np.pi),
                                         0.25 if i % 2 == 0 else 0.0, ALU.mult, ALU.add)
            link(last)
            link(dve.tensor_scalar(turn_n, turn_n, ROUNDER, None, ALU.add))
            link(dve.tensor_scalar(turn_n, turn_n, -ROUNDER, None, ALU.add))
            for part in TWO_PI_PARTS:
                link(dve.scalar_tensor_tensor(out=angle, in0=turn_n, scalar=-part, in1=angle, op0=ALU.mult,
                                              op1=ALU.add))
            split(2)
            for i in (0, 2):
                last = dve.tensor_scalar(chunks(angle, i, 1), chunks(angle, i, 1), float(np.pi / 2), None, ALU.add)
            link(last)
            dve.tensor_scalar(tab[:, :], angle, PI_IN, -PI_IN, ALU.min, ALU.max).then_inc(rows_ready, 1)
            rows.add()
            split(NU - 4)
            token_norm(r_main, D, True)
            dve.wait_ge(func_ready, funcs.add())
            for i, s in enumerate((sin_w, sin_n)):
                last = dve.tensor_scalar(s, s, con[:, C_FREQ + 2 + i:C_FREQ + 3 + i], None, ALU.mult)
            link(last)

            take_scaled(NU, tmp_a[:, :], r_main)
            low_gained(tmp_a, (mix_hi, mix_lo), 0, "g_q_lat")
            split(NU)
            token_norm(r_aux, Q_LAT)
            take_scaled(NU, tmp_a[:, :], r_main)
            low_gained(tmp_a, (mix_hi, mix_lo), 0, "g_kv_lat", n=KV_LAT // P, first=CB)
            link(dve.tensor_tensor(chunks(tmp_a, 2, 2), chunks(tmp_a, 2, 2), chunks(tab, 2, 2), ALU.mult))
            for half in range(2):
                rows_ = slice(half * P // 2, (half + 1) * P // 2)
                last = dve.tensor_tensor(chunks(heads, KR + half, 1)[rows_, :], chunks(tmp_a, 2, 1)[rows_, :],
                                         chunks(tmp_a, 3, 1)[rows_, :], ALU.add)
            last.then_inc(heads_ready, 1)
            split(NU)
            token_norm(r_kv, KV_LAT, True)
            take_scaled(NU, tmp_a[:, :], r_main)
            rotate(chunks(heads, DQ), cos_w, sin_w)
            for b in range(1, 4):
                split(NU)
                take_scaled(NU, tmp_a[:, :], r_main)
                rotate(chunks(heads, DQ + b * CB), cos_w, sin_w)
            for b in range(2):
                split(NU)
                take_token_major(NU, DV, 8 * P, b, r_main)
            for b in range(2):
                split(2)
                take_scaled(2, chunks(heads, QN + b * CB), r_aux)
            split(2)
            take_scaled(2, tmp_a[:, :], r_aux)
            rotate(chunks(heads, QR), cos_n, sin_n)
            for b in range(2):
                split(1)
                take_scaled(1, chunks(heads, KN + b * CB), r_kv)
            for b in range(2):
                split(1)
                take_token_major(1, MV, 8 * P, b, r_kv)
            attend(len(FIRST_JOBS), {
                7: lambda: mean_squares(chunks(heads, DV), both_pt, 2 * P, EPS_DIFF),
                8: diff_scale,
                10: lambda: kept_low(8, chunks(heads, DQ, 8))})

            clear_sums(tmp_c)
            for m in range(N_MEM):
                dve.engine_nop().then_inc(rows_ready, 1)
                rows.add()
                src = next_raw()
                add_squares()
                low_gained(src, (norm_hi, norm_lo), m, "g_mem", done=raw_read)
            split(NU)
            token_norm(r_aux, D, True)
            take_scaled(NU, chunks(heads, XK), r_aux)
            split(NU)
            take_token_major(NU, XV, 4 * P, 0, r_aux)
            residual(NU, "g_xattn")
            split(NU)
            token_norm(r_main, D)
            take_scaled(NU, chunks(heads, XQ), r_main)
            attend(len(CROSS_JOBS))
            residual(CB // UK, "g_ffn")
            mlp(None)

            split(NU)
            token_norm(r_aux, D, True)
            dve.wait_ge(sums_done, sums.add())
            dve.tensor_scalar(r_main[:, :], po[:, 1, 0:T + TT], 1.0 / D, None, ALU.mult).then_inc(ms_ready, 1)
            link(dve.tensor_tensor(r_kv[:, :], r_aux[:, :], r_aux[:, :], ALU.mult))
            link(dve.tensor_tensor(r_main[:, :], r_main[:, :], r_kv[:, :], ALU.mult))
            dve.tensor_scalar(r_main[:, :], r_main[:, :], EPS, None, ALU.add).then_inc(rows_ready, 1)
            dve.wait_ge(rows_ready, rows.add())
            root_ready_of(r_main[:, :])
            link(dve.tensor_tensor(r_main[:, :], r_main[:, :], r_aux[:, :], ALU.mult))
            take_scaled(NU, tmp_a[:, :], r_main)
            dve.wait_ge(tab_landed, 16)
            for b in range(4):
                split(3)
                mean_squares(tmp_b[:, :], both_pt, P, EPS)
                split(1)
                root_ready_of(tmp_b[:, :])
                dve.scalar_tensor_tensor(out=tmp_a[:, :], in0=tmp_a[:, :],
                                         scalar=gain("q_norm_2" if b < 2 else "k_norm_2", 0), in1=tmp_b[:, :],
                                         op0=ALU.mult, op1=ALU.mult).then_inc(rows_ready, 1)
                dve.wait_ge(rows_ready, rows.add())
                split(2)
                rotate(chunks(heads, AQ + b * CB), cos_w, sin_w)
                split(2)
                if b < 3:
                    take_scaled(NU, tmp_a[:, :], r_main)
            for b in range(2):
                take_token_major(NU, AV, 8 * P, b, r_main)
                for c in range(KC // 2 * b, KC // 2 * (b + 1)):
                    xs = chunks(x, c, 1)
                    dve.scalar_tensor_tensor(out=xs, in0=xs, scalar=gain("g_final", c), in1=r_aux[:, 0:T],
                                             op0=ALU.mult, op1=ALU.mult)
                if b == 0:
                    split(NU)
            with turns(dve, 2, {units: 2 * NU, raws: 2 * NU, ends: 2 * NU, taken: 2, swaps: 2, own: 2}) as i:
                for j in range(2):
                    split(NU)
                    take_scaled(NU, tmp_a[:, :], r_main)
                    rotate(block_of(heads, i * 2 + (RQ // CB + j)), cos_n, sin_n)
            for b in range(2):
                split(NU)
                take_token_major(NU, RV, 8 * P, b, r_main)
            for b in range(2):
                split(NU)
                take_scaled(NU, tmp_a[:, :], r_main)
                dve.wait_ge(func_ready, funcs.add())
                dve.tensor_tensor(chunks(heads, RG + b * CB), tmp_a[:, :], tmp_b[:, :], ALU.mult)\
                    .then_inc(heads_ready, 1)
            attend(len(SECOND_JOBS), {
                5: lambda: mean_squares(chunks(heads, RK), both_pt, P, EPS),
                6: lambda: ret_scale(0),
                8: lambda: kept_low(8, chunks(heads, RQ)),
                9: lambda: mean_squares(chunks(heads, RK + 4), both_pt, P, EPS),
                10: lambda: ret_scale(1),
                12: lambda: kept_low(12, chunks(heads, RQ + 4))})
            residual(NU, "g_ffn_2")
            mlp("g_ple_2")

            src = next_raw()
            low(mix_lo[:, 0:2 * T], src[:, 0:2 * T], mix_hi[:, 0:2 * T], raw_read)
            for b in range(NBD):
                split(1)
                took(dve.tensor_copy(block_of(heads, b), block_end(1)))
            for b in range(NBD):
                split(NU)
                if b == 0:
                    token_norm(r_main, D)
                take_scaled(NU, tmp_a[:, :], r_main)
                dve.wait_ge(func_ready, funcs.add())
                link(dve.tensor_tensor(tmp_b[:, :], tmp_b[:, :], block_of(heads, b), ALU.mult))
                dve.tensor_tensor(block_of(x, b), block_of(x, b), tmp_b[:, :], ALU.add).then_inc(out_ready, 1)
            assert units.fixed == UNITS and raws.fixed == RAWS


def weight_units(w, columns=None):
    if columns is not None:
        w = w[:, columns]
    k, n = w.shape
    return w.reshape(k // P // UK, UK, P, n // NB, NB).transpose(3, 0, 2, 1, 4).reshape(-1, P, UE)


def chunked(a):
    t, f = a.shape
    return a.T.reshape(f // P, P, t).transpose(1, 0, 2).reshape(P, -1)


def mlp_units(gate, up, down):
    parts, b0 = [], 0
    for n in GROUPS:
        g = weight_units(gate[:, b0 * NB:(b0 + n) * NB]).reshape(n, -1, P, UE)
        u = weight_units(up[:, b0 * NB:(b0 + n) * NB]).reshape(n, -1, P, UE)
        parts += [part for pair in zip(g, u) for part in pair]
        parts.append(weight_units(down[b0 * NB:(b0 + n) * NB]))
        b0 += n
    return parts


def by_head(start, heads, stride, first, width):
    return np.concatenate([start + h * stride + first + np.arange(width) for h in range(heads)])


def decays():
    gamma = 1.0 - 2.0 ** (-5.0 - np.arange(R_H))
    rel = np.arange(T)[None, :] - np.arange(T)[:, None]
    d = np.where(rel >= 0, gamma[:, None, None] ** np.maximum(rel, 0), 0.0) * P ** -0.5
    return d.reshape(R_H // 2, 2, TT, P, T).transpose(0, 3, 1, 2, 4).reshape(R_H // 2, P, UE).astype(np.float32)


def stream_of(a):
    rope0 = Q_LAT + KV_LAT
    rope = rope0 + np.arange(ROPE)
    partner = rope0 + (np.arange(ROPE) + ROPE // 2) % ROPE
    in_cols = np.concatenate([np.arange(rope0), rope, rope, partner, partner,
                              np.arange(rope0 + ROPE, rope0 + ROPE + 3 * 1024)])
    uq_cols = np.concatenate([by_head(0, MLA_H, NOPE + ROPE, 0, NOPE), by_head(0, MLA_H, NOPE + ROPE, NOPE, ROPE)])
    ukv_cols = np.concatenate([by_head(0, MLA_H, 2 * P, 0, P), by_head(0, MLA_H, 2 * P, P, P)])
    ukv = a["w_ukv"][0][:, ukv_cols]
    parts = [weight_units(a["w_in"][0], in_cols), weight_units(a["w_uq"][0], uq_cols), weight_units(ukv),
             weight_units(a["w_xk"][0]), weight_units(a["w_xv"][0]), weight_units(a["w_out"][0]),
             weight_units(a["w_xq"][0]), weight_units(a["w_xo"][0]),
             *mlp_units(a["w_gate"][0], a["w_up"][0], a["w_down"][0]),
             weight_units(a["w_in_2"][0]), weight_units(a["w_o_2"][0]),
             *mlp_units(a["w_gate_2"][0], a["w_up_2"][0], a["w_down_2"][0]),
             weight_units(a["w_ple_proj_2"][0]), weight_units(a["w_ple_gate_2"][0])]
    w = np.concatenate(parts)
    assert len(w) == UNITS
    mem = chunked(a["mem"][0]).reshape(P, N_MEM, UE).transpose(1, 0, 2)
    p = chunked(a["p_2"][0, 0])
    p = np.concatenate([p, p], axis=1)[None]
    return np.concatenate([w[:AT_MEM], mem, w[AT_MEM:AT_DECAY], decays(), w[AT_DECAY:AT_P], p, w[AT_P:]])


def vectors_of(a):
    return np.concatenate([np.asarray(a[name]).reshape(n, P).T for name, n in VECTORS], axis=1)


def frequencies(dim):
    return THETA ** -(np.arange(0, dim, 2) / dim)


def constants():
    con = np.zeros((P, C_N), np.float32)
    con[:, C_IDENT:C_IDENT + P] = np.eye(P)
    con[:, C_MASK:C_MASK + P] = np.where(np.arange(P)[None, :] > np.arange(P)[:, None], NEG, 0.0)
    p = np.arange(P)
    con[:, C_FREQ] = frequencies(P)[p % (P // 2)]
    con[:, C_FREQ + 1] = frequencies(ROPE)[p % (ROPE // 2)]
    con[:, C_FREQ + 2] = np.where(p < P // 2, -1.0, 1.0)
    con[:, C_FREQ + 3] = np.where(p % ROPE < ROPE // 2, -1.0, 1.0)
    return con


def second_tables():
    sign = np.where(np.arange(P) < P // 2, -1.0, 1.0)[:, None]
    out = []
    for freq in (frequencies(P), THETA ** -np.linspace(0.0, 1.0, P // 2)):
        freq = freq.astype(np.float32)[np.arange(P) % (P // 2)][:, None]
        angle = (np.arange(T, dtype=np.float32)[None, :] * freq).astype(np.float64)
        out += [np.cos(angle), sign * np.sin(angle)]
    return np.concatenate(out, axis=1).astype(np.float32)


def kernel(**inputs):
    import concourse.bacc as bacc
    from concourse.bass_utils import run_bass_kernel_spmd

    a = {name: np.asarray(value) for name, value in inputs.items()}
    arrays = {
        "stream": stream_of(a), "x_in": chunked(a["x"][0]), "vectors": vectors_of(a), "consts": constants(),
        "tables": second_tables(), "positions": a["positions"][0],
    }
    nc = bacc.Bacc("TRN2", target_bir_lowering=False, num_devices=1)
    aps = []
    for name, value in arrays.items():
        arrays[name] = value = np.ascontiguousarray(value)
        aps.append(nc.dram_tensor(name, value.shape, mybir.dt.from_np(value.dtype), kind="ExternalInput").ap())
    out = nc.dram_tensor("out", (P, KC * T), F32, kind="ExternalOutput").ap()
    two_blocks(nc, *aps, out)
    got = run_bass_kernel_spmd(nc, [arrays], core_ids=[0]).results[0]["out"]
    return np.ascontiguousarray(got.reshape(P, KC, T).transpose(2, 1, 0).reshape(1, T, D))
```

```python
from contextlib import ExitStack, contextmanager

import numpy as np

import concourse.bass as bass
from concourse import mybir

F32 = mybir.dt.float32
F32R = mybir.dt.float32r
I32 = mybir.dt.int32
ALU = mybir.AluOpType
ACT = mybir.ActivationFunctionType
AX = mybir.AxisListType

P = 128
T = 256
TT = T // P
D = 2048
KC = D // P
CB = 4
NB = CB * P
UK = 2
UE = UK * NB
RING = 4
MLA_H, NOPE, ROPE, Q_LAT, KV_LAT = 8, 128, 64, 512, 256
DIFF_H = 4
X_H = 4
A_H = R_H = 8
HID = 5632
PLE = 256
GROUPS = (4, 4, 3)
assert sum(GROUPS) * NB == HID and max(GROUPS) * CB <= KC
LAMBDA_INIT = 0.8 - 0.6 * 1.0
EPS = 1e-6
EPS_DIFF = 1e-5
NEG = -1e30
BCOLS = CB * T

VECTORS = (("g_mix", KC), ("g_q_lat", Q_LAT // P), ("g_kv_lat", KV_LAT // P), ("g_xattn", KC), ("g_mem", KC),
           ("g_ffn", KC), ("g_final", KC), ("g_mix_2", KC), ("g_ffn_2", KC), ("g_ple_2", KC),
           ("b_ple_gate_2", KC), ("g_ret_2", R_H), ("g_diff_sub", 2), ("q_norm_2", 1), ("k_norm_2", 1),
           ("lambda_q1", 1), ("lambda_q2", 1), ("lambda_k1", 1), ("lambda_k2", 1))
VCOL = {}
for _name, _n in VECTORS:
    VCOL[_name] = sum(n for m, n in VECTORS[:len(VCOL)])
VN = sum(n for _, n in VECTORS)
VCOL["g_both"] = VN

THETA = 10000.0
ROUNDER = 1.5 * 2.0 ** 23
TWO_PI_1 = 6.28125
TWO_PI_2 = round((2 * np.pi - TWO_PI_1) * 2 ** 20) / 2 ** 20
TWO_PI_PARTS = (TWO_PI_1, TWO_PI_2, float(2 * np.pi - TWO_PI_1 - TWO_PI_2))
PI_IN = 3.1415925

C_IDENT, C_MASK, C_FREQ, C_N = 0, P, 2 * P, 2 * P + 4

U_IN = (Q_LAT + 512 + 3 * 1024) // NB * (KC // UK)
U_UQ = 3 * (Q_LAT // P // UK)
U_UKV = 4 * (KV_LAT // P // UK)
U_X = KC // UK
U_RES = D // NB * (KC // UK)
U_XO = D // NB * (CB // UK)
U_MLP = 2 * sum(GROUPS) * (KC // UK) + sum(D // NB * g * CB // UK for g in GROUPS)
U_IN2 = 14 * (KC // UK)
U_PLE = D // NB * (PLE // P // UK)
UNITS = U_IN + U_UQ + U_UKV + 2 * U_X + U_RES + U_X + U_XO + U_MLP + U_IN2 + U_PLE + U_RES + U_MLP + U_RES
AT_MEM = U_IN + U_UQ + U_UKV + RING
AT_DECAY = AT_MEM - RING + 2 * U_X + U_RES + U_X + U_XO + U_MLP + U_IN2 + RING
AT_P = AT_DECAY
N_MEM, N_DECAY, N_P = D * T // P // UE, R_H // 2, 1
RAWS = UNITS + N_MEM + N_DECAY + N_P


class Tally:

    def __init__(self):
        self.fixed, self.per, self.turn = 0, 0, None

    def add(self, n=1):
        self.fixed += n
        return self.value()

    def value(self, back=0):
        if self.turn is None:
            return self.fixed - back
        return self.turn * self.per + (self.fixed - back)


@contextmanager
def turns(engine, n, counts):
    start = {tally: tally.fixed for tally in counts}
    with engine.Fori(0, n) as turn:
        for tally, per in counts.items():
            tally.turn, tally.per = turn, per
        yield turn
    for tally, per in counts.items():
        assert tally.fixed - start[tally] == per, (tally.fixed - start[tally], per)
        tally.fixed += (n - 1) * per
        tally.turn = None


FIRST_JOBS = [("diff", h) for h in range(DIFF_H)] + [("mla", h) for h in range(MLA_H)]
CROSS_JOBS = [("cross", h) for h in range(X_H)]
SECOND_JOBS = [("ret", h) for h in range(R_H)] + [("moba", h) for h in range(A_H)]
JOBS = FIRST_JOBS + CROSS_JOBS + SECOND_JOBS
SCALE = {"mla": (NOPE + ROPE) ** -0.5, "diff": P ** -0.5, "cross": P ** -0.5, "moba": P ** -0.5}


def slot_of(n):
    return (n + (n < len(FIRST_JOBS))) % 2


def nth(n, kinds):
    return sum(kind in kinds for kind, _ in JOBS[:n + 1])


SOFT = ("diff", "mla", "cross", "moba")
KEPT = ("diff", "ret")
SPLIT = ("mla", "cross", "moba")


def outputs_at(n0, n_jobs, step):
    return [n for n in range(n0, n0 + n_jobs) if n - n0 + (1 if JOBS[n][0] == "ret" else 3) == step]


def two_blocks(nc: bass.Bass, stream, x_in, vectors, consts, tables, positions, out):
    with ExitStack() as ctx:
        def sb(name, shape, dt=F32):
            return ctx.enter_context(nc.sbuf_tensor(name, shape, dt))

        def sem(name):
            return ctx.enter_context(nc.semaphore(name))

        raw = sb("raw", [P, RING, UE])
        w_hi = sb("w_hi", [P, RING, UE], F32R)
        w_lo = sb("w_lo", [P, RING, UE], F32R)
        x = sb("x", [P, KC * T])
        norm_hi = sb("norm_hi", [P, KC * T], F32R)
        norm_lo = sb("norm_lo", [P, KC * T], F32R)
        mix_hi = sb("mix_hi", [P, KC * T], F32R)
        mix_lo = sb("mix_lo", [P, KC * T], F32R)
        heads = sb("heads", [P, 14 * BCOLS])
        tmp_a = sb("tmp_a", [P, BCOLS])
        tmp_b = sb("tmp_b", [P, BCOLS])
        tmp_c = sb("tmp_c", [P, BCOLS])
        tmp_d = sb("tmp_d", [P, BCOLS])
        tab = sb("tab", [P, 4 * T])
        vec = sb("vec", [P, VN + KC])
        con = sb("con", [P, C_N])
        ones = sb("ones", [P, P])
        r_main = sb("r_main", [P, T + TT])
        r_aux = heads[:, 54 * T:55 * T + TT]
        r_kv = tmp_d[:, 0:T + TT]
        r_head = sb("r_head", [P, 4 * TT])
        lam = sb("lam", [P, 4])
        nmax = sb("nmax", [P, 3, 4])
        rowsum = sb("rowsum", [P, 3, 4])

        acc = ctx.enter_context(nc.psum_tensor("acc", [P, 2, BCOLS], F32))
        pt = ctx.enter_context(nc.psum_tensor("pt", [P, 2, 2 * T], F32))
        po = ctx.enter_context(nc.psum_tensor("po", [P, 2, 2 * T], F32))

        raw_landed = [sem(f"raw_landed{i}") for i in range(RING)]
        x_landed = [sem(f"x_landed{i}") for i in range(D // NB)]
        vec_landed = sem("vec_landed")
        con_landed = sem("con_landed")
        tab_landed = sem("tab_landed")
        ones_ready = sem("ones_ready")
        out_stored = sem("out_stored")
        w_hi_ready = sem("w_hi_ready")
        raw_read = sem("raw_read")
        w_used = sem("w_used")
        block_taken = sem("block_taken")
        rows_ready = sem("rows_ready")
        squares_ready = sem("squares_ready")
        tile_squares = sem("tile_squares")
        sums_ready = sem("sums_ready")
        sums_done = sem("sums_done")
        ms_ready = sem("ms_ready")
        root_ready = sem("root_ready")
        inverse_ready = sem("inverse_ready")
        hi_ready = sem("hi_ready")
        kept_hi_ready = sem("kept_hi_ready")
        operand_ready = sem("operand_ready")
        swap_ready = sem("swap_ready")
        func_ready = sem("func_ready")
        heads_ready = sem("heads_ready")
        scores_done = sem("scores_done")
        nmax_ready = sem("nmax_ready")
        exp_ready = sem("exp_ready")
        probs_ready = sem("probs_ready")
        trans_done = sem("trans_done")
        probsT_ready = sem("probsT_ready")
        decayed_ready = sem("decayed_ready")
        head_done = sem("head_done")
        kept_ready = sem("kept_ready")
        head_split = sem("head_split")
        lam_ready = sem("lam_ready")
        out_ready = sem("out_ready")
        act_done = sem("act_done")
        dve_done = sem("dve_done")

        def chunks(t, first, n=CB):
            return t[:, first * T:(first + n) * T]

        def block_of(t, b):
            return t[:, bass.ds(b * BCOLS, BCOLS)]

        def by_chunk(ap):
            return ap.rearrange("p (c t) -> p c t", c=CB)

        def over_chunks(row):
            return row.rearrange("p (o t) -> p o t", o=1).broadcast_to([P, CB, T])

        def gain(name, c):
            return vec[:, bass.ds(c + VCOL[name], 1)]

        ident = con[:, C_IDENT:C_IDENT + P]
        mask = con[:, C_MASK:C_MASK + P]
        cos_w, sin_w = tab[:, 0:T], tab[:, T:2 * T]
        cos_n, sin_n = tab[:, 2 * T:3 * T], tab[:, 3 * T:4 * T]
        probs = (tmp_a, tmp_b, tmp_d)
        both_pt = pt[:, :, :].rearrange("p a b -> p (a b)")

        DQ, DK, DV, QN, QR, KN, MV, KR = 0, 8, 16, 24, 32, 36, 44, 52
        XK, XV, XQ = 0, 4, 8
        AQ, AK, AV, RQ, RK, RV, RG = 0, 8, 16, 24, 32, 40, 48
        PP = 0
        NU = KC // UK
        NBD = D // NB
        ROTATED_FIRST, ROTATED_SECOND = 6, 8 + 2

        block = ctx.enter_context(nc.Block())

        @block.sync
        def _(sp):
            def load(r, slot):
                sp.dma_start(raw[:, slot, :], stream[bass.ds(r, 1)].rearrange("o p n -> (o p) n"))\
                    .then_inc(raw_landed[slot], 16)

            def load_x(b):
                sp.dma_start(block_of(x, b), block_of(x_in, b)).then_inc(x_landed[b], 16)

            for b in range(NBD):
                load_x(b)
                if b < RING // 2:
                    load(2 * b, 2 * b)
                    load(2 * b + 1, 2 * b + 1)
            with sp.Fori(0, RAWS // RING - 1) as i:
                for s in range(RING):
                    sp.wait_ge(raw_read, i * RING + (s + 1))
                    load(i * RING + (RING + s), s)
            for r in range(RAWS // RING * RING, RAWS):
                sp.wait_ge(raw_read, r - RING + 1)
                load(r, r % RING)
            for b in range(NBD):
                sp.wait_ge(out_ready, b + 1)
                sp.dma_start(block_of(out, b), block_of(x, b)).then_inc(out_stored, 16)
            sp.wait_ge(out_stored, 16 * NBD)

        @block.gpsimd
        def _(pool):
            pool.dma_start(con[:, :], consts).then_inc(con_landed, 16)
            pool.dma_start(tmp_b[:, 0:T].bitcast(I32), positions.rearrange("(o t) -> o t", o=1).broadcast_to([P, T]))\
                .then_inc(con_landed, 16)
            pool.wait_ge(heads_ready, ROTATED_FIRST)
            pool.dma_start(tab[:, :], tables).then_inc(tab_landed, 16)

        @block.tensor
        def _(pe):
            units, blocks, operands, seen, tiles, means, rotated, spreads = (Tally() for _ in range(8))
            job = [0]
            norm, mix = (norm_hi, norm_lo), (mix_hi, mix_lo)

            def unit_split():
                u = units.fixed - 1
                extra = (u >= AT_MEM) * N_MEM + (u >= AT_DECAY) * N_DECAY + (u >= AT_P) * N_P
                return units.value() + extra

            def one_block(n_units, act, k0=0, token_major=False, need=None, mid=None, mid_at=5, part=None):
                part = part or range(n_units)
                mids = mid if isinstance(mid, dict) else {mid_at: mid} if mid else {}
                act_hi, act_lo = act
                if part[0] == 0:
                    blocks.add()
                slot = (blocks.fixed - 1) % 2
                if part[0] == 0 and blocks.fixed > 2:
                    pe.wait_ge(block_taken, blocks.value(2))
                for ki in part:
                    units.add()
                    s = (units.fixed - 1) % RING
                    pe.wait_ge(raw_read, unit_split())
                    if need:
                        pe.wait_ge(*need(ki))
                    for c in range(TT if token_major else CB):
                        for kk in range(UK):
                            k = k0 + ki * UK + kk
                            clear = ki == 0 and kk == 0 and (token_major or c % 2 == 0)
                            if token_major:
                                order = ((w_hi, act_hi), (w_lo, act_hi), (w_hi, act_lo))
                            else:
                                order = ((w_hi, act_hi), (w_hi, act_lo), (w_lo, act_hi))
                            for i, (w, a) in enumerate(order):
                                if token_major:
                                    last = pe.matmul(acc[:, slot, c * NB:(c + 1) * NB],
                                                     a[:, k * T + c * P:k * T + (c + 1) * P],
                                                     w[:, s, kk * NB:(kk + 1) * NB], start=clear and i == 0,
                                                     stop=ki == n_units - 1, skip_group_check=True)
                                else:
                                    last = pe.matmul(acc[:, slot, c * T:(c + 1) * T],
                                                     w[:, s, kk * NB + c * P:kk * NB + (c + 1) * P],
                                                     a[:, k * T:(k + 1) * T], start=clear and i == 0,
                                                     stop=ki == n_units - 1, skip_group_check=True)
                    last.then_inc(w_used, 1)
                    if ki in mids:
                        mids[ki]()

            def released(n):
                if n >= 0:
                    kind = JOBS[n][0]
                    if kind in KEPT:
                        pe.wait_ge(kept_ready, nth(n, KEPT))
                    else:
                        pe.wait_ge(head_split, nth(n, SPLIT))

            def means_read():
                if means.fixed:
                    pe.wait_ge(ms_ready, means.fixed)

            def token_sums(src, n, ready=None, bank=0, both=False):
                if bank == 0:
                    means_read()
                released(job[0] - 1)
                released(job[0] - 2)
                if ready:
                    pe.wait_ge(*ready)
                for c in range(n):
                    last = pe.matmul(po[:, bank, 0:T], ones[:, :], src[:, c * T:(c + 1) * T],
                              start=c == 0, stop=c == n - 1, skip_group_check=True)
                for t in range(TT if both else 0):
                    for c in range(n):
                        last = pe.matmul(po[:, bank, T + t:T + t + 1], src[:, c * T + t * P:c * T + (t + 1) * P],
                                         ones[:, 0:1], start=False, stop=c == n - 1, skip_group_check=True)
                last.then_inc(sums_done, 1)
                means.add()

            def added_sums(both=False, src=tmp_c, n=NBD):
                return lambda: token_sums(src, 1, (sums_ready, seen.add(n + 1)), both=both)

            def tile_sums(n, both=False):
                return lambda: token_sums(tmp_c, n, (tile_squares, tiles.add()), both=both)

            def transposed_read():
                means_read()
                if job[0]:
                    pe.wait_ge(probsT_ready, nth(transposed[0], SOFT))

            def head_sums(src, per=1):
                pe.wait_ge(tile_squares, tiles.add())
                transposed_read()
                for h in range(4):
                    for t in range(TT):
                        for c in range(per):
                            at = (h * per + c) * T + t * P
                            last = pe.matmul(pt[:, 0, h * TT + t:h * TT + t + 1], src[:, at:at + P], ones[:, 0:1],
                                             start=h == 0 and t == 0 and c == 0, stop=c == per - 1,
                                             skip_group_check=True)
                last.then_inc(sums_done, 1)
                means.add()

            def spread():
                pe.wait_ge(inverse_ready, spreads.add())
                transposed_read()
                for h in range(4):
                    for t in range(TT):
                        at = h % 2 * T + t * P
                        last = pe.matmul(pt[:, h // 2, at:at + P],
                                         r_head[:, h * TT + t:h * TT + t + 1].broadcast_to([P, P]), ident,
                                         start=h % 2 == 0 and t == 0, stop=True, skip_group_check=True)
                last.then_inc(sums_done, 1)
                means.add()

            transposed = [-1]

            def operand_need(base):
                return lambda ki: (operand_ready, base + ki * UK // CB + 1)

            def residual(n_units, act, need=None, mid=None, peel=False):
                if mid or peel:
                    one_block(n_units, act, need=need, mid=mid)
                    one_block(n_units, act)
                with turns(pe, NBD // 2 - bool(mid or peel), {units: 2 * n_units, blocks: 2}):
                    for _ in range(2):
                        one_block(n_units, act, need=None if mid or peel else need)

            def mlp(need):
                for g, n in enumerate(GROUPS):
                    if g == 0:
                        one_block(NU, norm, need=need, mid=added_sums())
                        one_block(NU, norm)
                    with turns(pe, n - (g == 0), {units: 2 * NU, blocks: 2}):
                        one_block(NU, norm)
                        one_block(NU, norm)
                    down = operand_need(operands.fixed)
                    operands.add(n)
                    nd = n * CB // UK
                    with turns(pe, NBD // 2, {units: 2 * nd, blocks: 2}):
                        for _ in range(2):
                            one_block(nd, mix, need=down)

            def scores(n):
                kind, h = JOBS[n]
                slot = slot_of(n)
                if n >= 2:
                    if JOBS[n - 2][0] == "ret":
                        pe.wait_ge(decayed_ready, nth(n - 2, ("ret",)))
                    else:
                        pe.wait_ge(exp_ready, nth(n - 2, SOFT))
                if kind == "ret":
                    for kk in range(TT):
                        last = pe.matmul(acc[:, slot, kk * (T + P):(kk + 1) * T],
                                         heads[:, (RK + h) * T + kk * P:(RK + h) * T + (kk + 1) * P],
                                         heads[:, (RQ + h) * T + kk * P:(RQ + h + 1) * T],
                                         start=kk == 0, stop=True, skip_group_check=True)
                    last.then_inc(scores_done, 1)
                    return
                for comp in range(2 if kind == "diff" else 1):
                    parts = {"diff": [(DQ + 2 * h + comp, DK + 2 * h + comp)],
                             "mla": [(QN + h, KN + h), (QR + h // 2, KR + h % 2)],
                             "cross": [(XQ + h, XK + h)], "moba": [(AQ + h, AK + h)]}[kind]
                    for t in range(TT):
                        width = (t + 1) * P if kind == "moba" else T
                        for i, (q, k) in enumerate(parts):
                            at = (comp * TT + t) * T
                            last = pe.matmul(acc[:, slot, at:at + width],
                                             heads[:, q * T + t * P:q * T + (t + 1) * P],
                                             heads[:, k * T:k * T + width], start=t == 0 and i == 0,
                                             stop=i == len(parts) - 1, skip_group_check=True)
                last.then_inc(scores_done, 1)

            def transposes(n):
                kind, h = JOBS[n]
                if kind == "ret":
                    return
                pe.wait_ge(probs_ready, nth(n, SOFT))
                if n >= 2 and nth(n - 2, SOFT):
                    pe.wait_ge(probsT_ready, nth(n - 2, SOFT))
                means_read()
                prob = probs[n % 3]
                for kk in range(TT):
                    for t in range(kk if kind == "moba" else 0, TT):
                        last = pe.transpose(pt[:, n % 2, kk * T + t * P:kk * T + (t + 1) * P],
                                            prob[:, t * T + kk * P:t * T + (kk + 1) * P], ident)
                last.then_inc(trans_done, 1)
                transposed[0] = n

            def values(n):
                kind, h = JOBS[n]
                if kind == "ret":
                    pe.wait_ge(decayed_ready, nth(n, ("ret",)))
                else:
                    pe.wait_ge(probsT_ready, nth(n, SOFT))
                released(n - 2)
                means_read()
                prob_t = tmp_c[:, n % 2 * 2 * T:(n % 2 + 1) * 2 * T]
                first, width, wide = {"diff": (DV, 8 * P, 2), "mla": (MV, 8 * P, 1), "cross": (XV, 4 * P, 1),
                                      "ret": (RV, 8 * P, 1), "moba": (AV, 8 * P, 1)}[kind]
                for e in range(wide):
                    for kk in range(TT):
                        q0 = kk * P if kind in ("ret", "moba") else 0
                        v = first * T + kk * width + (h * wide + e) * P
                        last = pe.matmul(po[:, n % 2, e * T + q0:(e + 1) * T], heads[:, v:v + P],
                                         prob_t[:, kk * T + q0:(kk + 1) * T], start=kk == 0 and e == 0,
                                         stop=kk == TT - 1, skip_group_check=True)
                last.then_inc(head_done, 1)
                job[0] = n + 1

            def first_scores():
                assert slot_of(job[0]) == blocks.fixed % 2
                pe.wait_ge(block_taken, blocks.fixed - 1)
                pe.wait_ge(heads_ready, rotated.fixed)
                scores(job[0])

            def attend(n_jobs, at=None, after=None, started=False):
                n0 = job[0]
                pe.wait_ge(block_taken, blocks.fixed)
                for i in range(n_jobs + 3):
                    if started <= i < n_jobs:
                        scores(n0 + i)
                    if at and i in at:
                        at[i]()
                    if 2 <= i < n_jobs + 2:
                        transposes(n0 + i - 2)
                    for n in outputs_at(n0, n_jobs, i):
                        values(n)
                    if after and i in after:
                        after[i]()

            pe.wait_ge(lam_ready, 1)
            pe.matmul(po[:, 1, 0:2], ones[:, :], lam[:, 0:2], start=True, stop=True).then_inc(sums_done, 1)

            one_block(NU, norm, need=operand_need(0), mid=added_sums(True))
            one_block(NU, norm, mid=tile_sums(Q_LAT // P))
            one_block(NU, norm, mid=tile_sums(KV_LAT // P, True))
            one_block(NU, norm)
            one_block(NU, norm)
            one_block(NU, norm)
            operands.add(NBD + 2)
            for _ in range(2):
                one_block(Q_LAT // P // UK, mix, need=lambda ki: (operand_ready, NBD + 2))
            for i in range(4):
                one_block(1, mix, k0=CB, token_major=i >= 2)
            one_block(Q_LAT // P // UK, mix)
            rotated.add(ROTATED_FIRST)
            one_block(NU, norm, token_major=True)
            one_block(NU, norm, token_major=True, mid=first_scores, mid_at=3)

            def memory_keys(part, mid=None):
                if part[0] == 0:
                    pe.wait_ge(exp_ready, len(FIRST_JOBS))
                one_block(NU, norm, need=lambda ki: (raw_read, AT_MEM + ki * UK // CB + 1), mid=mid, part=part)

            last_step = len(FIRST_JOBS) + 2
            attend(len(FIRST_JOBS), {7: lambda: head_sums(chunks(heads, DK, 8), 2), },
                   {9: spread, last_step - 2: lambda: memory_keys(range(0, 1)), last_step - 1: lambda: memory_keys(range(1, 2))},
                   started=True)
            memory_keys(range(2, NU), added_sums(True, chunks(heads, DV), 2 * N_MEM - 1))
            one_block(NU, norm, token_major=True)
            operands.add(1)
            pe.wait_ge(operand_ready, operands.fixed)
            pe.wait_ge(head_split, MLA_H)
            residual(NU, mix)
            one_block(NU, norm, need=operand_need(operands.fixed), mid=added_sums())
            operands.add(NBD)
            attend(len(CROSS_JOBS))
            residual(CB // UK, mix, need=lambda ki: (head_split, MLA_H + UK * (ki + 1)))
            need = operand_need(operands.fixed)
            operands.add(NBD)
            mlp(need)

            def both_sums():
                token_sums(tmp_c, 1, (sums_ready, seen.add(2 * NBD + 2)), both=True)
                token_sums(tmp_b, 1, bank=1, both=True)

            one_block(NU, norm, need=operand_need(operands.fixed), mid=both_sums, mid_at=3)
            operands.add(NBD)
            for b in range(1, 5):
                one_block(NU, norm, token_major=b == 4, mid={1: lambda: head_sums(tmp_b), 3: spread})
            one_block(NU, norm, token_major=True)
            with turns(pe, 2, {units: 2 * NU, blocks: 2}):
                one_block(NU, norm)
                one_block(NU, norm)
            rotated.add(ROTATED_SECOND)
            one_block(NU, norm)
            one_block(NU, norm)
            one_block(NU, norm, token_major=True)
            one_block(NU, norm, token_major=True, mid=first_scores)

            def embedding():
                pe.wait_ge(exp_ready, nth(len(JOBS), SOFT))
                one_block(1, norm, need=lambda ki: (raw_read, AT_P + N_MEM + N_DECAY + N_P))

            last_step = len(SECOND_JOBS) + 2
            attend(len(SECOND_JOBS), {5: lambda: head_sums(chunks(heads, RK)), 7: spread,
                                      9: lambda: head_sums(chunks(heads, RK + 4))},
                   {11: spread, last_step - 2: embedding, last_step - 1: embedding, last_step: embedding}, started=True)
            embedding()
            operands.add(2)
            pe.wait_ge(operand_ready, operands.fixed)
            pe.wait_ge(head_split, nth(len(JOBS), SPLIT))
            residual(NU, mix, peel=True)
            need = operand_need(operands.fixed)
            operands.add(NBD)
            mlp(need)

            residual(NU, norm, need=operand_need(operands.fixed), mid=added_sums())
            assert units.fixed == UNITS

        @block.scalar
        def _(act):
            raws, units, taken, rows, means, nmaxs = (Tally() for _ in range(6))
            job = [0]

            def take_raw():
                raws.add()
                at = raws.fixed - 1
                turn = at // RING + 1
                if raws.turn is not None:
                    turn = raws.turn * (raws.per // RING) + turn
                act.wait_ge(raw_landed[at % RING], turn * 16)
                return raw[:, at % RING, :]

            def split(n):
                for _ in range(n):
                    if units.turn is None and units.fixed == UNITS:
                        return
                    src = take_raw()
                    units.add()
                    if units.fixed > RING:
                        act.wait_ge(w_used, units.value(RING))
                    act.activation(w_hi[:, (units.fixed - 1) % RING, :], src, ACT.Copy).then_inc(w_hi_ready, 1)

            def roots(r):
                act.wait_ge(ms_ready, means.add())
                act.activation(r, r, ACT.Sqrt).then_inc(root_ready, 1)

            def split_with_root(r):
                split(NU - 2)
                roots(r)
                split(2)

            def wait_taken(n=1):
                act.wait_ge(block_taken, taken.add(n))

            def wait_rows():
                act.wait_ge(rows_ready, rows.add())

            def hi_gained(src, dst, b, name, n=CB):
                for c in range(n):
                    last = act.activation(dst[:, bass.ds(b * BCOLS + c * T, T)], src[:, c * T:(c + 1) * T], ACT.Copy,
                                          scale=gain(name, b * CB + c))
                last.then_inc(hi_ready, 1)

            def squares(src):
                act.activation(tmp_a[:, :], src, ACT.Square).then_inc(squares_ready, 1)

            def swap(half):
                for a in range(0, P, 2 * half):
                    act.activation(tmp_b[a:a + half, :], tmp_a[a + half:a + 2 * half, :], ACT.Copy)
                    last = act.activation(tmp_b[a + half:a + 2 * half, :], tmp_a[a:a + half, :], ACT.Copy)
                last.then_inc(swap_ready, 1)

            def residual_block(b, name):
                wait_taken()
                squares(block_of(x, b))
                hi_gained(block_of(x, b), norm_hi, b, name)

            def residual(n_units, name, peel=0):
                for b in range(peel):
                    split(n_units)
                    residual_block(b, name)
                with turns(act, (NBD - peel) // 2, {units: 2 * n_units, raws: 2 * n_units, taken: 2}) as i:
                    for j in range(2):
                        split(n_units)
                        residual_block(i * 2 + (j + peel), name)

            def mlp(last_gain):
                def pair(i, first=False):
                    if first:
                        split_with_root(r_main[:, 0:T])
                    else:
                        split(NU)
                    wait_taken()
                    act.activation(tmp_b[:, :], tmp_a[:, :], ACT.Sigmoid).then_inc(func_ready, 1)
                    split(NU)
                    taken.add()
                    wait_rows()
                    act.activation(block_of(mix_hi, i), tmp_b[:, :], ACT.Copy).then_inc(hi_ready, 1)

                for g, n in enumerate(GROUPS):
                    nd = n * CB // UK
                    first = int(g == 0)
                    if first:
                        pair(0, True)
                    with turns(act, n - first, {units: 2 * NU, raws: 2 * NU, taken: 2, rows: 1}) as i:
                        pair(i + first)
                    if g < len(GROUPS) - 1:
                        with turns(act, NBD // 2, {units: 2 * nd, raws: 2 * nd, taken: 2}):
                            split(2 * nd)
                            taken.add(2)
                    elif last_gain:
                        residual(nd, last_gain)
                    else:
                        for b in range(NBD):
                            split(nd)
                            wait_taken()
                            squares(block_of(x, b))
                            for c in range(CB):
                                last = act.activation(chunks(tmp_d, c, 1), chunks(x, b * CB + c, 1), ACT.Square,
                                                      scale=gain("g_final", b * CB + c))
                            last.then_inc(squares_ready, 1)
                            hi_gained(block_of(x, b), norm_hi, b, "g_both")

            def exps(n):
                kind, h = JOBS[n]
                if kind == "ret":
                    return
                if n >= 3 and JOBS[n - 3][0] in SOFT:
                    act.wait_ge(trans_done, nth(n - 3, SOFT))
                act.wait_ge(nmax_ready, nth(n, SOFT))
                prob = probs[n % 3]
                for i in range(2 * TT if kind == "diff" else TT):
                    width = (i + 1) * P if kind == "moba" else T
                    last = act.activation(prob[:, i * T:i * T + width], acc[:, slot_of(n), i * T:i * T + width], ACT.Exp,
                                          bias=nmax[:, n % 3, i:i + 1], scale=SCALE[kind],
                                          accum_out=rowsum[:, n % 3, i:i + 1])
                last.then_inc(exp_ready, 1)

            def copy_transposed(n):
                kind, h = JOBS[n]
                if kind == "ret":
                    return
                act.wait_ge(trans_done, nth(n, SOFT))
                if n >= 2:
                    act.wait_ge(head_done, n - 1)
                dst = tmp_c[:, n % 2 * 2 * T:(n % 2 + 1) * 2 * T]
                if kind == "moba":
                    act.activation(dst[:, 0:T], pt[:, n % 2, 0:T], ACT.Copy)
                    last = act.activation(dst[:, T + P:], pt[:, n % 2, T + P:], ACT.Copy)
                else:
                    last = act.activation(dst, pt[:, n % 2, :], ACT.Copy)
                last.then_inc(probsT_ready, 1)

            def keep(n):
                kind, h = JOBS[n]
                act.wait_ge(head_done, n + 1)
                if kind == "diff":
                    act.activation(chunks(heads, DQ + 2 * h, 2), po[:, n % 2, :], ACT.Copy).then_inc(kept_ready, 1)
                elif kind == "ret":
                    act.activation(chunks(heads, RQ + h, 1), po[:, n % 2, 0:T], ACT.Copy).then_inc(kept_ready, 1)
                else:
                    act.activation(chunks(mix_hi, h, 1), po[:, n % 2, 0:T], ACT.Copy).then_inc(hi_ready, 1)

            def attend(n_jobs, at=None, started=False):
                n0 = job[0]
                for i in range(n_jobs + 3):
                    if 2 <= i < n_jobs + 2:
                        copy_transposed(n0 + i - 2)
                    if started <= i < n_jobs:
                        exps(n0 + i)
                    for n in outputs_at(n0, n_jobs, i):
                        keep(n)
                    if at and i in at:
                        at[i]()
                job[0] += n_jobs

            def head_squares(src, dst, kept):
                act.wait_ge(kept_ready, kept)
                act.activation(dst, src, ACT.Square).then_inc(tile_squares, 1)

            def wait_scaled():
                act.wait_ge(ms_ready, means.add())

            def head_hi(first, src, wait=wait_scaled):
                wait()
                act.activation(chunks(mix_hi, first, src.shape[1] // T), src, ACT.Copy).then_inc(kept_hi_ready, 1)

            def load_table(func):
                act.activation(r_head[:, 0:1], ones[:, 0:1], func)

            act.dma_start(vec[:, 0:VN], vectors).then_inc(vec_landed, 16)
            act.wait_ge(ones_ready, 1)
            load_table(ACT.Copy)
            act.wait_ge(vec_landed, 16)

            def start_hi(b):
                act.wait_ge(x_landed[b], 16)
                hi_gained(block_of(x, b), norm_hi, b, "g_mix")

            def start_squares(b):
                if b:
                    act.wait_ge(sums_ready, b)
                squares(block_of(x, b))

            for b in range(2):
                start_hi(b)
                split(2)
            for b in range(NBD):
                if b < 2:
                    start_hi(b + 2)
                start_squares(b)
                split(1)
            wait_rows()
            act.activation(lam[:, 2:4], lam[:, 2:4], ACT.Exp).then_inc(func_ready, 1)

            split(2)
            roots(r_main[:, :])
            split(2)
            wait_taken()
            act.activation(tmp_c[:, :], tmp_a[:, :], ACT.Square).then_inc(tile_squares, 1)
            hi_gained(tmp_a, mix_hi, 0, "g_q_lat")
            split(4)
            wait_rows()
            act.activation(tab[:, :], tab[:, :], ACT.Sin).then_inc(func_ready, 1)
            split(2)
            roots(r_aux[:, 0:T])
            split(2)
            wait_taken()
            act.activation(tmp_c[:, 0:2 * T], tmp_a[:, 0:2 * T], ACT.Square).then_inc(tile_squares, 1)
            for c in range(KV_LAT // P):
                last = act.activation(chunks(mix_hi, CB + c, 1), chunks(tmp_a, c, 1), ACT.Copy,
                                      scale=gain("g_kv_lat", c))
            last.then_inc(hi_ready, 1)
            split_with_root(r_kv[:, :])
            wait_taken()
            swap(P // 2)
            for _ in range(3):
                split(NU)
                wait_taken()
                swap(P // 2)
            split(4 + 4)
            taken.add(6)
            split(2)
            wait_taken()
            swap(ROPE // 2)
            split(NU)
            taken.add(2)
            split(4)
            exps(0)
            split(4)

            def memory(m):
                hi_gained(take_raw(), norm_hi, m, "g_mem")

            attend(len(FIRST_JOBS), {
                6: lambda: head_squares(chunks(heads, DQ, 8), chunks(heads, DK, 8), DIFF_H),
                7: lambda: (roots(r_head[:, :]), memory(0)),
                10: lambda: head_hi(8, chunks(heads, DQ, 8)),
                9: lambda: memory(1), 11: lambda: memory(2), 12: lambda: memory(3)},
                   started=True)
            split_with_root(r_aux[:, :])
            taken.add(2)
            split(NU)
            residual(NU, "g_xattn")
            split_with_root(r_main[:, 0:T])
            load_table(ACT.Exp)
            taken.add()
            attend(len(CROSS_JOBS))
            residual(CB // UK, "g_ffn")
            mlp(None)

            split(4)
            roots(r_aux[:, :])
            split(2)
            means.add()
            wait_rows()
            act.activation(r_main[:, :], r_main[:, :], ACT.Sqrt).then_inc(root_ready, 1)
            split(2)
            for b in range(4):
                wait_taken()
                act.activation(tmp_b[:, :], tmp_a[:, :], ACT.Square).then_inc(tile_squares, 1)
                split(2)
                roots(r_head[:, :])
                split(2)
                wait_scaled()
                swap(P // 2)
                split(4)
            taken.add(2)
            split(NU)
            with turns(act, 4, {units: NU, raws: NU, taken: 1}):
                split(NU)
                wait_taken()
                swap(P // 2)
            for b in range(2):
                split(NU)
                wait_taken()
                act.activation(tmp_b[:, :], tmp_a[:, :], ACT.Sigmoid).then_inc(func_ready, 1)
            split(2 * NU)
            taken.add(2 + NBD)

            def embedding():
                src = take_raw()
                act.activation(norm_hi[:, 0:2 * T], src[:, 0:2 * T], ACT.Copy).then_inc(hi_ready, 1)

            raws.add(N_DECAY)
            ret_kept = DIFF_H + 4
            attend(len(SECOND_JOBS), {
                4: lambda: head_squares(chunks(heads, RQ), chunks(heads, RK), ret_kept),
                5: lambda: roots(r_head[:, :]),
                8: lambda: (means.add(), head_hi(8, chunks(heads, RQ), wait_rows),
                            head_squares(chunks(heads, RQ + 4), chunks(heads, RK + 4), ret_kept + 4)),
                9: lambda: roots(r_head[:, :]),
                12: lambda: (means.add(), head_hi(12, chunks(heads, RQ + 4), wait_rows)),
                13: embedding, 17: lambda: split(1), 18: lambda: split(1)}, started=True)
            split(2)
            residual(NU, "g_ffn_2")
            mlp("g_ple_2")

            for b in range(NBD):
                if b == 0:
                    split_with_root(r_main[:, 0:T])
                else:
                    split(NU)
                wait_taken()
                for c in range(CB):
                    last = act.activation(chunks(tmp_b, c, 1), chunks(tmp_a, c, 1), ACT.Sigmoid,
                                          bias=gain("b_ple_gate_2", b * CB + c))
                last.then_inc(func_ready, 1)
            assert units.fixed == UNITS and raws.fixed == RAWS

        @block.vector
        def _(dve):
            (raws, units, ends, taken, his, squared, added, sums, roots_n, swaps, funcs, rows, own,
             kept_his, means) = (Tally() for _ in range(15))
            job = [0]

            def link(ins):
                ins.then_inc(dve_done, 1)
                dve.wait_ge(dve_done, own.add())

            def next_raw():
                raws.add()
                return raw[:, (raws.fixed - 1) % RING, :]

            def split(n):
                for _ in range(n):
                    if units.turn is None and units.fixed == UNITS:
                        return
                    src = next_raw()
                    dve.wait_ge(w_hi_ready, units.add())
                    s = (units.fixed - 1) % RING
                    dve.tensor_tensor(w_lo[:, s, :], src, w_hi[:, s, :].bitcast(F32), ALU.subtract)\
                        .then_inc(raw_read, 1)

            def block_end(n_units):
                dve.wait_ge(w_used, ends.add(n_units))
                taken.add()
                return acc[:, (taken.fixed - 1) % 2, :]

            def took(ins):
                ins.then_inc(block_taken, 1)
                dve.wait_ge(block_taken, taken.value())

            def take_scaled(n_units, dst, r):
                src = block_end(n_units)
                took(dve.tensor_tensor(by_chunk(dst), by_chunk(src), over_chunks(r[:, 0:T]), ALU.mult))

            def take_token_major(n_units, first, width, b, r):
                src = block_end(n_units)
                for t in range(TT):
                    at = first * T + t * width + b * NB
                    last = dve.tensor_scalar(heads[:, at:at + NB], src[:, t * NB:(t + 1) * NB],
                                             r[:, T + t:T + t + 1], None, ALU.mult)
                took(last)

            def take_added(n_units, b):
                src = block_end(n_units)
                took(dve.tensor_tensor(block_of(x, b), block_of(x, b), src, ALU.add))

            def root_ready_of(r):
                dve.wait_ge(root_ready, roots_n.add())
                link(dve.reciprocal(r, r))

            def mean_squares(r, src, count, eps):
                dve.wait_ge(sums_done, sums.add())
                dve.tensor_scalar(r, src, 1.0 / count, eps, ALU.mult, ALU.add).then_inc(ms_ready, 1)
                means.add()

            def head_mean_squares(count, eps):
                mean_squares(r_head[:, :], pt[:, 0, 0:4 * TT], count, eps)

            def head_inverses(factor=None):
                dve.wait_ge(root_ready, roots_n.add())
                ins = dve.reciprocal(r_head[:, :], r_head[:, :])
                if factor is not None:
                    link(ins)
                    ins = dve.tensor_scalar(r_head[:, :], r_head[:, :], factor, None, ALU.mult)
                ins.then_inc(inverse_ready, 1)

            def scaled(ins):
                ins.then_inc(ms_ready, 1)
                dve.wait_ge(ms_ready, means.add())

            def token_norm(r, count, both=False):
                w = T + TT if both else T
                mean_squares(r[:, 0:w], po[:, 0, 0:w], count, EPS)
                root_ready_of(r[:, 0:w])

            def split_with_norm(r, count, both=False, late=0):
                split(NU - 2)
                token_norm(r, count, both)
                split(2 - late)

            def add_squares(src=tmp_a, dst=tmp_c):
                dve.wait_ge(squares_ready, squared.add())
                if added.fixed:
                    dve.wait_ge(sums_ready, added.value())
                dve.tensor_tensor(dst[:, :], dst[:, :], src[:, :], ALU.add).then_inc(sums_ready, 1)
                added.add()

            def fold_squares(sums):
                dve.wait_ge(sums_ready, added.value())
                link(dve.tensor_tensor(chunks(sums, 0, 2), chunks(sums, 0, 2), chunks(sums, 2, 2), ALU.add))
                dve.tensor_tensor(chunks(sums, 0, 1), chunks(sums, 0, 1), chunks(sums, 1, 1), ALU.add)\
                    .then_inc(sums_ready, 1)
                added.add()

            def low(dst, src, hi, done=operand_ready):
                dve.wait_ge(hi_ready, his.add())
                dve.tensor_tensor(dst, src, hi.bitcast(F32), ALU.subtract).then_inc(done, 1)

            def low_gained(src, dst, b, name, n=CB, first=0, done=operand_ready):
                dve.wait_ge(hi_ready, his.add())
                dst_hi, dst_lo = dst
                for c in range(n):
                    at = bass.ds(b * BCOLS + (first + c) * T, T)
                    last = dve.scalar_tensor_tensor(out=dst_lo[:, at], in0=src[:, c * T:(c + 1) * T],
                                                    scalar=gain(name, b * CB + c), in1=dst_hi[:, at].bitcast(F32),
                                                    op0=ALU.mult, op1=ALU.subtract)
                last.then_inc(done, 1)

            def rotate(dst, cos, sin):
                dve.tensor_tensor(by_chunk(dst), by_chunk(tmp_a[:, :]), over_chunks(cos), ALU.mult)
                dve.wait_ge(swap_ready, swaps.add())
                link(dve.tensor_tensor(by_chunk(tmp_b[:, :]), by_chunk(tmp_b[:, :]), over_chunks(sin), ALU.mult))
                dve.tensor_tensor(dst, dst, tmp_b[:, :], ALU.add).then_inc(heads_ready, 1)

            def clear_sums(*which):
                for t in which:
                    link(dve.memset(t[:, :], 0.0))

            def residual_block(n_units, b, name):
                split(n_units - 1)
                take_added(n_units, b)
                split(1)
                add_squares()
                low_gained(block_of(x, b), (norm_hi, norm_lo), b, name)

            def residual(n_units, name):
                clear_sums(tmp_c)
                with turns(dve, NBD // 2, {units: 2 * n_units, raws: 2 * n_units, ends: 2 * n_units, taken: 2,
                                           squared: 2, added: 2, his: 2}) as i:
                    for j in range(2):
                        residual_block(n_units, i * 2 + j, name)
                fold_squares(tmp_c)

            def mlp(last_gain):
                def pair(i, first=False):
                    if first:
                        split_with_norm(r_main, D)
                    else:
                        split(NU)
                    take_scaled(NU, tmp_a[:, :], r_main)
                    split(NU)
                    dve.wait_ge(func_ready, funcs.add())
                    link(dve.tensor_tensor(tmp_a[:, :], tmp_a[:, :], tmp_b[:, :], ALU.mult))
                    take_scaled(NU, tmp_b[:, :], r_main)
                    dve.tensor_tensor(tmp_b[:, :], tmp_b[:, :], tmp_a[:, :], ALU.mult).then_inc(rows_ready, 1)
                    dve.wait_ge(rows_ready, rows.add())
                    low(block_of(mix_lo, i), tmp_b[:, :], block_of(mix_hi, i))

                for g, n in enumerate(GROUPS):
                    nd = n * CB // UK
                    first = int(g == 0)
                    if first:
                        pair(0, True)
                    with turns(dve, n - first, {units: 2 * NU, raws: 2 * NU, ends: 2 * NU, taken: 2, funcs: 1,
                                                own: 1, rows: 1, his: 1}) as i:
                        pair(i + first)
                    if g < len(GROUPS) - 1:
                        with turns(dve, NBD // 2, {units: 2 * nd, raws: 2 * nd, ends: 2 * nd, taken: 2}) as i:
                            for j in range(2):
                                split(nd)
                                take_added(nd, i * 2 + j)
                    elif last_gain:
                        residual(nd, last_gain)
                    else:
                        clear_sums(tmp_c, tmp_b)
                        with turns(dve, NBD // 2, {units: 2 * nd, raws: 2 * nd, ends: 2 * nd, taken: 2, squared: 4,
                                                   added: 4, his: 2}) as i:
                            for j in range(2):
                                b = i * 2 + j
                                split(nd - 1)
                                take_added(nd, b)
                                split(1)
                                add_squares()
                                add_squares(tmp_d, tmp_b)
                                low_gained(block_of(x, b), (norm_hi, norm_lo), b, "g_both")
                        fold_squares(tmp_c)
                        fold_squares(tmp_b)

            def maxima(n):
                kind, h = JOBS[n]
                dve.wait_ge(scores_done, n + 1)
                s = acc[:, slot_of(n), :]
                if kind == "ret":
                    if h % 2 == 0:
                        src = next_raw()
                        at = raws.fixed - 1
                        dve.wait_ge(raw_landed[at % RING], 16 * (at // RING + 1))
                        decay[0] = src
                    if n >= 2:
                        dve.wait_ge(head_done, n - 1)
                    dst = tmp_c[:, n % 2 * 2 * T:(n % 2 + 1) * 2 * T]
                    d = decay[0][:, h % 2 * 2 * T:(h % 2 + 1) * 2 * T]
                    dve.tensor_tensor(dst[:, 0:T], s[:, 0:T], d[:, 0:T], ALU.mult)
                    dve.tensor_tensor(dst[:, T + P:], s[:, T + P:2 * T], d[:, T + P:], ALU.mult)\
                        .then_inc(decayed_ready, 1)
                    if h == R_H - 1:
                        dve.wait_ge(decayed_ready, R_H)
                        dve.sem_inc(raw_read, N_DECAY)
                    return
                w = 2 * TT if kind == "diff" else TT
                m = nmax[:, n % 3, 0:w]
                if kind == "moba":
                    for t in range(TT):
                        diag = s[:, t * (T + P):t * (T + P) + P]
                        last = dve.tensor_tensor(diag, diag, mask, ALU.add)
                    link(last)
                    for t in range(TT):
                        last = dve.tensor_reduce(nmax[:, n % 3, t:t + 1], s[:, t * T:t * T + (t + 1) * P], AX.X, ALU.max)
                    link(last)
                else:
                    link(dve.tensor_reduce(m, s[:, 0:w * T].rearrange("p (i t) -> p i t", i=w), AX.X, ALU.max))
                dve.tensor_scalar(m, m, -SCALE[kind], None, ALU.mult).then_inc(nmax_ready, 1)

            decay = [None]

            def normalise(n):
                kind, h = JOBS[n]
                if kind == "ret":
                    return
                dve.wait_ge(exp_ready, nth(n, SOFT))
                prob = probs[n % 3]
                w = 2 * TT if kind == "diff" else TT
                sum_ = rowsum[:, n % 3, :]
                link(dve.reciprocal(sum_[:, 0:w], sum_[:, 0:w]))
                if kind == "diff":
                    link(dve.tensor_scalar(sum_[:, TT:w], sum_[:, TT:w], lam[:, 0:1], None, ALU.mult))
                    for t in range(TT):
                        p2 = chunks(prob, TT + t, 1)
                        last = dve.tensor_scalar(p2, p2, sum_[:, TT + t:TT + t + 1], None, ALU.mult)
                    link(last)
                    for t in range(TT):
                        last = dve.scalar_tensor_tensor(out=chunks(prob, t, 1), in0=chunks(prob, t, 1),
                                                        scalar=sum_[:, t:t + 1], in1=chunks(prob, TT + t, 1),
                                                        op0=ALU.mult, op1=ALU.add)
                else:
                    for t in range(TT):
                        p = prob[:, t * T:t * T + ((t + 1) * P if kind == "moba" else T)]
                        last = dve.tensor_scalar(p, p, sum_[:, t:t + 1], None, ALU.mult)
                last.then_inc(probs_ready, 1)

            def split_head(n):
                kind, h = JOBS[n]
                if kind in SPLIT:
                    low(chunks(mix_lo, h, 1), po[:, n % 2, 0:T], chunks(mix_hi, h, 1), head_split)

            def attend(n_jobs, at=None, started=False):
                n0 = job[0]
                for i in range(n_jobs + 4):
                    if started <= i < n_jobs:
                        maxima(n0 + i)
                    if 1 + started <= i <= n_jobs:
                        normalise(n0 + i - 1)
                    for n in outputs_at(n0, n_jobs, i - 1):
                        split_head(n)
                    if at and i in at:
                        at[i]()
                job[0] += n_jobs

            def diff_scale():
                dve.wait_ge(sums_done, sums.add())
                for e in range(2):
                    o = chunks(heads, DQ, 8).rearrange("p (h e t) -> p e h t", h=DIFF_H, e=2)[:, e]
                    last = dve.scalar_tensor_tensor(out=o, in0=o, scalar=gain("g_diff_sub", e), in1=by_chunk(both_pt),
                                                    op0=ALU.mult, op1=ALU.mult)
                scaled(last)

            def ret_scale(half):
                o, g = chunks(heads, RQ + 4 * half), chunks(heads, RG + 4 * half)
                dve.wait_ge(sums_done, sums.add())
                for c in range(4):
                    last = dve.scalar_tensor_tensor(out=chunks(o, c, 1), in0=chunks(o, c, 1),
                                                    scalar=gain("g_ret_2", 4 * half + c), in1=chunks(both_pt, c, 1),
                                                    op0=ALU.mult, op1=ALU.mult)
                scaled(last)
                dve.tensor_tensor(o, o, g, ALU.mult).then_inc(rows_ready, 1)
                dve.wait_ge(rows_ready, rows.add())

            def kept_low(first, src):
                n = src.shape[1] // T
                dve.wait_ge(kept_hi_ready, kept_his.add())
                dve.tensor_tensor(chunks(mix_lo, first, n), src, chunks(mix_hi, first, n).bitcast(F32), ALU.subtract)\
                    .then_inc(operand_ready, 1)

            dve.memset(ones[:, :], 1.0).then_inc(ones_ready, 1)
            dve.memset(chunks(heads, KR, 1)[P // 2:P, :], 0.0)
            dve.memset(chunks(heads, KR + 1, 1)[0:P // 2, :], 0.0)
            clear_sums(tmp_c)
            dve.wait_ge(vec_landed, 16)
            dve.tensor_tensor(lam[:, 0:2], vec[:, VCOL["lambda_q1"]:VCOL["lambda_q1"] + 2],
                              vec[:, VCOL["lambda_k1"]:VCOL["lambda_k1"] + 2], ALU.mult).then_inc(lam_ready, 1)
            dve.tensor_tensor(vec[:, VCOL["g_both"]:VCOL["g_both"] + KC], vec[:, VCOL["g_final"]:VCOL["g_final"] + KC],
                              vec[:, VCOL["g_mix_2"]:VCOL["g_mix_2"] + KC], ALU.mult)
            for b in range(2):
                low_gained(block_of(x, b), (norm_hi, norm_lo), b, "g_mix")
                split(2)
            for b in range(NBD):
                if b < 2:
                    low_gained(block_of(x, b + 2), (norm_hi, norm_lo), b + 2, "g_mix")
                add_squares()
                if b == NBD - 1:
                    fold_squares(tmp_c)
                split(1)
            dve.wait_ge(sums_done, sums.add())
            dve.tensor_copy(lam[:, 2:4], po[:, 1, 0:2]).then_inc(rows_ready, 1)
            dve.wait_ge(rows_ready, rows.add())

            dve.wait_ge(con_landed, 32)
            pos, angle, turn_n = heads[:, 0:T], heads[:, BCOLS:2 * BCOLS], heads[:, 2 * BCOLS:3 * BCOLS]
            link(dve.tensor_copy(pos, tmp_b[:, 0:T].bitcast(I32)))
            for i in range(4):
                last = dve.tensor_scalar(chunks(angle, i, 1), pos, con[:, C_FREQ + i // 2:C_FREQ + i // 2 + 1], None,
                                         ALU.mult)
            link(last)
            dve.wait_ge(func_ready, funcs.add())
            link(dve.tensor_tensor(lam[:, 0:1], lam[:, 3:4], lam[:, 2:3], ALU.subtract))
            link(dve.tensor_scalar(lam[:, 0:1], lam[:, 0:1], -LAMBDA_INIT, None, ALU.add))
            split(2)
            token_norm(r_main, D, True)
            split(2)

            take_scaled(NU, tmp_a[:, :], r_main)
            low_gained(tmp_a, (mix_hi, mix_lo), 0, "g_q_lat")
            for i in range(4):
                last = dve.tensor_scalar(chunks(turn_n, i, 1), chunks(angle, i, 1), 1.0 / (2 * np.pi),
                                         0.25 if i % 2 == 0 else 0.0, ALU.mult, ALU.add)
            link(last)
            link(dve.tensor_scalar(turn_n, turn_n, ROUNDER, None, ALU.add))
            split(1)
            link(dve.tensor_scalar(turn_n, turn_n, -ROUNDER, None, ALU.add))
            for part in TWO_PI_PARTS:
                split(1)
                link(dve.scalar_tensor_tensor(out=angle, in0=turn_n, scalar=-part, in1=angle, op0=ALU.mult,
                                              op1=ALU.add))
            for i in (0, 2):
                last = dve.tensor_scalar(chunks(angle, i, 1), chunks(angle, i, 1), float(np.pi / 2), None, ALU.add)
            link(last)
            dve.tensor_scalar(tab[:, :], angle, PI_IN, -PI_IN, ALU.min, ALU.max).then_inc(rows_ready, 1)
            rows.add()
            split(2)
            token_norm(r_aux, Q_LAT)
            split(2)
            dve.wait_ge(func_ready, funcs.add())
            for i, s in enumerate((sin_w, sin_n)):
                last = dve.tensor_scalar(s, s, con[:, C_FREQ + 2 + i:C_FREQ + 3 + i], None, ALU.mult)
            link(last)
            take_scaled(NU, tmp_a[:, :], r_main)
            low_gained(tmp_a, (mix_hi, mix_lo), 0, "g_kv_lat", n=KV_LAT // P, first=CB)
            link(dve.tensor_tensor(chunks(tmp_a, 2, 2), chunks(tmp_a, 2, 2), chunks(tab, 2, 2), ALU.mult))
            for half in range(2):
                rows_ = slice(half * P // 2, (half + 1) * P // 2)
                last = dve.tensor_tensor(chunks(heads, KR + half, 1)[rows_, :], chunks(tmp_a, 2, 1)[rows_, :],
                                         chunks(tmp_a, 3, 1)[rows_, :], ALU.add)
            last.then_inc(heads_ready, 1)
            split_with_norm(r_kv, KV_LAT, True)
            take_scaled(NU, tmp_a[:, :], r_main)
            rotate(chunks(heads, DQ), cos_w, sin_w)
            for b in range(1, 4):
                split(NU)
                take_scaled(NU, tmp_a[:, :], r_main)
                rotate(chunks(heads, DQ + b * CB), cos_w, sin_w)
            for b in range(2):
                split(1)
                take_scaled(2, chunks(heads, QN + b * CB), r_aux)
                split(1)
            for b in range(2):
                split(1)
                take_scaled(1, chunks(heads, KN + b * CB), r_kv)
            for b in range(2):
                split(1)
                take_token_major(1, MV, 8 * P, b, r_kv)
            split(2)
            take_scaled(2, tmp_a[:, :], r_aux)
            rotate(chunks(heads, QR), cos_n, sin_n)
            split(NU)
            take_token_major(NU, DV, 8 * P, 0, r_main)
            split(4)
            maxima(0)
            split(2)
            normalise(0)
            split(1)
            take_token_major(NU, DV, 8 * P, 1, r_main)
            split(1)
            mem_sums, mem_squares = chunks(heads, DV), chunks(heads, DV + CB)

            def memory(m):
                src = next_raw()
                dve.wait_ge(hi_ready, his.fixed + 1)
                if m:
                    dve.wait_ge(sums_ready, added.value())
                dve.tensor_tensor(mem_squares if m else mem_sums, src, src, ALU.mult).then_inc(sums_ready, 1)
                added.add()
                if m:
                    dve.wait_ge(sums_ready, added.value())
                    dve.tensor_tensor(mem_sums, mem_sums, mem_squares, ALU.add).then_inc(sums_ready, 1)
                    added.add()
                low_gained(src, (norm_hi, norm_lo), m, "g_mem", done=raw_read)
                if m == N_MEM - 1:
                    fold_squares(mem_sums)

            attend(len(FIRST_JOBS), {
                7: lambda: head_mean_squares(2 * P, EPS_DIFF),
                8: lambda: (head_inverses(1.0 - LAMBDA_INIT), memory(0)),
                9: diff_scale,
                10: lambda: memory(1), 11: lambda: kept_low(8, chunks(heads, DQ, 8)),
                12: lambda: memory(2), 13: lambda: memory(3)}, started=True)
            split_with_norm(r_aux, D, True)
            take_scaled(NU, chunks(heads, XK), r_aux)
            split(NU)
            take_token_major(NU, XV, 4 * P, 0, r_aux)
            residual(NU, "g_xattn")
            split_with_norm(r_main, D, late=1)
            take_scaled(NU, chunks(heads, XQ), r_main)
            split(1)
            attend(len(CROSS_JOBS))
            residual(CB // UK, "g_ffn")
            mlp(None)

            split(4)
            token_norm(r_aux, D, True)
            dve.wait_ge(sums_done, sums.add())
            dve.tensor_scalar(r_main[:, :], po[:, 1, 0:T + TT], 1.0 / D, None, ALU.mult).then_inc(ms_ready, 1)
            means.add()
            link(dve.tensor_tensor(r_kv[:, :], r_aux[:, :], r_aux[:, :], ALU.mult))
            link(dve.tensor_tensor(r_main[:, :], r_main[:, :], r_kv[:, :], ALU.mult))
            dve.tensor_scalar(r_main[:, :], r_main[:, :], EPS, None, ALU.add).then_inc(rows_ready, 1)
            dve.wait_ge(rows_ready, rows.add())
            split(2)
            root_ready_of(r_main[:, :])
            link(dve.tensor_tensor(r_main[:, :], r_main[:, :], r_aux[:, :], ALU.mult))
            split(2)
            take_scaled(NU, tmp_a[:, :], r_main)
            dve.wait_ge(tab_landed, 16)
            for b in range(4):
                split(2)
                head_mean_squares(P, EPS)
                split(1)
                head_inverses()
                split(1)
                dve.wait_ge(sums_done, sums.add())
                scaled(dve.scalar_tensor_tensor(out=tmp_a[:, :], in0=tmp_a[:, :],
                                                scalar=gain("q_norm_2" if b < 2 else "k_norm_2", 0), in1=both_pt,
                                                op0=ALU.mult, op1=ALU.mult))
                split(2)
                rotate(chunks(heads, AQ + b * CB), cos_w, sin_w)
                split(2)
                if b < 3:
                    take_scaled(NU, tmp_a[:, :], r_main)
            for b in range(2):
                take_token_major(NU, AV, 8 * P, b, r_main)
                for c in range(KC // 2 * b, KC // 2 * (b + 1)):
                    xs = chunks(x, c, 1)
                    dve.scalar_tensor_tensor(out=xs, in0=xs, scalar=gain("g_final", c), in1=r_aux[:, 0:T],
                                             op0=ALU.mult, op1=ALU.mult)
                if b == 0:
                    split(NU)
            with turns(dve, 2, {units: 2 * NU, raws: 2 * NU, ends: 2 * NU, taken: 2, swaps: 2, own: 2}) as i:
                for j in range(2):
                    split(NU)
                    take_scaled(NU, tmp_a[:, :], r_main)
                    rotate(block_of(heads, i * 2 + (RQ // CB + j)), cos_n, sin_n)
            for b in range(2):
                split(NU)
                take_scaled(NU, tmp_a[:, :], r_main)
                dve.wait_ge(func_ready, funcs.add())
                dve.tensor_tensor(chunks(heads, RG + b * CB), tmp_a[:, :], tmp_b[:, :], ALU.mult)\
                    .then_inc(heads_ready, 1)
            split(NU)
            take_token_major(NU, RV, 8 * P, 0, r_main)
            split(NU - 1)
            take_token_major(NU, RV, 8 * P, 1, r_main)
            split(1)
            maxima(job[0])

            def embedding_low():
                src = next_raw()
                low(norm_lo[:, 0:2 * T], src[:, 0:2 * T], norm_hi[:, 0:2 * T], raw_read)

            def embedding(b):
                split(1)
                took(dve.tensor_copy(block_of(heads, PP // CB + b), block_end(1)))

            attend(len(SECOND_JOBS), {
                5: lambda: head_mean_squares(P, EPS),
                6: head_inverses,
                7: lambda: ret_scale(0),
                9: lambda: (kept_low(8, chunks(heads, RQ)), head_mean_squares(P, EPS)),
                10: head_inverses,
                11: lambda: ret_scale(1),
                13: lambda: kept_low(12, chunks(heads, RQ + 4)), 14: embedding_low,
                17: lambda: embedding(0), 18: lambda: embedding(1), 19: lambda: embedding(2)}, started=True)
            embedding(3)
            residual(NU, "g_ffn_2")
            mlp("g_ple_2")

            for b in range(NBD):
                if b == 0:
                    split_with_norm(r_main, D)
                else:
                    split(NU)
                take_scaled(NU, tmp_a[:, :], r_main)
                dve.wait_ge(func_ready, funcs.add())
                link(dve.tensor_tensor(tmp_b[:, :], tmp_b[:, :], block_of(heads, b), ALU.mult))
                dve.tensor_tensor(block_of(x, b), block_of(x, b), tmp_b[:, :], ALU.add).then_inc(out_ready, 1)
            assert units.fixed == UNITS and raws.fixed == RAWS


def weight_units(w, columns=None):
    if columns is not None:
        w = w[:, columns]
    k, n = w.shape
    return w.reshape(k // P // UK, UK, P, n // NB, NB).transpose(3, 0, 2, 1, 4).reshape(-1, P, UE)


def chunked(a):
    t, f = a.shape
    return a.T.reshape(f // P, P, t).transpose(1, 0, 2).reshape(P, -1)


def mlp_units(gate, up, down):
    parts, b0 = [], 0
    for n in GROUPS:
        g = weight_units(gate[:, b0 * NB:(b0 + n) * NB]).reshape(n, -1, P, UE)
        u = weight_units(up[:, b0 * NB:(b0 + n) * NB]).reshape(n, -1, P, UE)
        parts += [part for pair in zip(g, u) for part in pair]
        parts.append(weight_units(down[b0 * NB:(b0 + n) * NB]))
        b0 += n
    return parts


def by_head(start, heads, stride, first, width):
    return np.concatenate([start + h * stride + first + np.arange(width) for h in range(heads)])


def decays():
    gamma = 1.0 - 2.0 ** (-5.0 - np.arange(R_H))
    rel = np.arange(T)[None, :] - np.arange(T)[:, None]
    d = np.where(rel >= 0, gamma[:, None, None] ** np.maximum(rel, 0), 0.0) * P ** -0.5
    return d.reshape(R_H // 2, 2, TT, P, T).transpose(0, 3, 1, 2, 4).reshape(R_H // 2, P, UE).astype(np.float32)


def stream_of(a):
    rope0 = Q_LAT + KV_LAT
    rope = rope0 + np.arange(ROPE)
    partner = rope0 + (np.arange(ROPE) + ROPE // 2) % ROPE
    in_cols = np.concatenate([np.arange(rope0), rope, rope, partner, partner,
                              np.arange(rope0 + ROPE, rope0 + ROPE + 3 * 1024)])
    uq_cols = np.concatenate([by_head(0, MLA_H, NOPE + ROPE, 0, NOPE), by_head(0, MLA_H, NOPE + ROPE, NOPE, ROPE)])
    ukv_cols = np.concatenate([by_head(0, MLA_H, 2 * P, 0, P), by_head(0, MLA_H, 2 * P, P, P)])
    ukv = a["w_ukv"][0][:, ukv_cols]
    w_in = weight_units(a["w_in"][0], in_cols)
    values = len(w_in) - 2 * (KC // UK)
    in2_cols = np.concatenate([np.arange(3 * 1024 + 2048), 6 * 1024 + np.arange(1024), 5 * 1024 + np.arange(1024)])
    w_uq = weight_units(a["w_uq"][0], uq_cols)
    rotated = len(w_uq) * 2 // 3
    parts = [w_in[:values], w_uq[:rotated], weight_units(ukv), w_uq[rotated:], w_in[values:],
             weight_units(a["w_xk"][0]), weight_units(a["w_xv"][0]), weight_units(a["w_out"][0]),
             weight_units(a["w_xq"][0]), weight_units(a["w_xo"][0]),
             *mlp_units(a["w_gate"][0], a["w_up"][0], a["w_down"][0]),
             weight_units(a["w_in_2"][0], in2_cols), weight_units(a["w_ple_proj_2"][0]), weight_units(a["w_o_2"][0]),
             *mlp_units(a["w_gate_2"][0], a["w_up_2"][0], a["w_down_2"][0]),
             weight_units(a["w_ple_gate_2"][0])]
    w = np.concatenate(parts)
    assert len(w) == UNITS
    mem = chunked(a["mem"][0]).reshape(P, N_MEM, UE).transpose(1, 0, 2)
    p = chunked(a["p_2"][0, 0])
    p = np.concatenate([p, p], axis=1)[None]
    return np.concatenate([w[:AT_MEM], mem, w[AT_MEM:AT_DECAY], decays(), p, w[AT_DECAY:]])


def vectors_of(a):
    return np.concatenate([np.asarray(a[name]).reshape(n, P).T for name, n in VECTORS], axis=1)


def frequencies(dim):
    return THETA ** -(np.arange(0, dim, 2) / dim)


def constants():
    con = np.zeros((P, C_N), np.float32)
    con[:, C_IDENT:C_IDENT + P] = np.eye(P)
    con[:, C_MASK:C_MASK + P] = np.where(np.arange(P)[None, :] > np.arange(P)[:, None], NEG, 0.0)
    p = np.arange(P)
    con[:, C_FREQ] = frequencies(P)[p % (P // 2)]
    con[:, C_FREQ + 1] = frequencies(ROPE)[p % (ROPE // 2)]
    con[:, C_FREQ + 2] = np.where(p < P // 2, -1.0, 1.0)
    con[:, C_FREQ + 3] = np.where(p % ROPE < ROPE // 2, -1.0, 1.0)
    return con


def second_tables():
    sign = np.where(np.arange(P) < P // 2, -1.0, 1.0)[:, None]
    out = []
    for freq in (frequencies(P), THETA ** -np.linspace(0.0, 1.0, P // 2)):
        freq = freq.astype(np.float32)[np.arange(P) % (P // 2)][:, None]
        angle = (np.arange(T, dtype=np.float32)[None, :] * freq).astype(np.float64)
        out += [np.cos(angle), sign * np.sin(angle)]
    return np.concatenate(out, axis=1).astype(np.float32)


def kernel(**inputs):
    import concourse.bacc as bacc
    from concourse.bass_utils import run_bass_kernel_spmd

    a = {name: np.asarray(value) for name, value in inputs.items()}
    arrays = {
        "stream": stream_of(a), "x_in": chunked(a["x"][0]), "vectors": vectors_of(a), "consts": constants(),
        "tables": second_tables(), "positions": a["positions"][0],
    }
    nc = bacc.Bacc("TRN2", target_bir_lowering=False, num_devices=1)
    aps = []
    for name, value in arrays.items():
        arrays[name] = value = np.ascontiguousarray(value)
        aps.append(nc.dram_tensor(name, value.shape, mybir.dt.from_np(value.dtype), kind="ExternalInput").ap())
    out = nc.dram_tensor("out", (P, KC * T), F32, kind="ExternalOutput").ap()
    two_blocks(nc, *aps, out)
    got = run_bass_kernel_spmd(nc, [arrays], core_ids=[0]).results[0]["out"]
    return np.ascontiguousarray(got.reshape(P, KC, T).transpose(2, 1, 0).reshape(1, T, D))
```
